# Optimizing a Trainium2 kernel written in Bass

```python
import math
import jax, jax.numpy as jnp
from jax import lax
import numpy as np

D_MODEL = 1024
BATCH = 1
SEQ = 256
DEPTH = 2

N_EVEN = (DEPTH + 1) // 2
N_ODD = DEPTH // 2
CHUNK = 64
CONV_K = 4
LN_EPS = 1e-5
NORM_EPS = 1e-6
RET_H = 4
RET_DK = D_MODEL // 8
RET_DV = D_MODEL // 4
ROPE_BASE = 10000.0
ML_H = 4
ML_DK = D_MODEL // 8
ML_DV = D_MODEL // 4
GLA_H = 4
GLA_DK = D_MODEL // 8
GLA_DV = D_MODEL // 4
GLA_RANK = 16
GLA_TAU = 16.0
SSD_HEADDIM = 64
SSD_DINNER = D_MODEL
SSD_H = SSD_DINNER // SSD_HEADDIM
SSD_GROUPS = 4
SSD_HPG = SSD_H // SSD_GROUPS
SSD_N = 128
N_EXPERTS = 16
N_EXPERT_GROUPS = 4
EXPERTS_PER_GROUP = N_EXPERTS // N_EXPERT_GROUPS
TOP_K = 2
GROUP_SCORE_TOPK = 2
D_FF = D_MODEL // 2
DEEPNORM_ALPHA = (2.0 * DEPTH) ** 0.25
DEEPNORM_BETA = (8.0 * DEPTH) ** -0.25
RET_SPLITS = (RET_H * RET_DK, RET_H * RET_DK, RET_H * RET_DV, RET_H * RET_DV)
ML_SPLITS = (ML_H * ML_DK, ML_H * ML_DK, ML_H * ML_DV, ML_H * ML_DV, ML_H, ML_H)
P_AB = sum(RET_SPLITS) + sum(ML_SPLITS)
MIX_AB = RET_H * RET_DV + ML_H * ML_DV
GLA_SPLITS = (GLA_H * GLA_DK, GLA_H * GLA_DK, GLA_H * GLA_DV, GLA_H * GLA_DV, GLA_RANK)
SSD_SPLITS = (SSD_DINNER, SSD_DINNER + 2 * SSD_GROUPS * SSD_N, SSD_H)
P_CD = sum(GLA_SPLITS) + sum(SSD_SPLITS)
MIX_CD = GLA_H * GLA_DV + SSD_DINNER

kernel_name = 'hybrid_retention_mlstm_gla_ssd_grouped_moe_deepnorm'

def _split(t, sizes):
    return jnp.split(t, np.cumsum(sizes)[:-1].tolist(), axis=-1)

def _heads(t, h):
    b, s, hd = t.shape
    return t.reshape(b, s, h, hd // h).transpose(0, 2, 1, 3)

def _chunks(t):
    b, h, s = t.shape[:3]
    return jnp.moveaxis(t.reshape(b, h, s // CHUNK, CHUNK, *t.shape[3:]), 2, 0)

def _unchunk(t):
    nc, b, h, c, d = t.shape
    return t.transpose(1, 0, 3, 2, 4).reshape(b, nc * c, h * d)

def _seq_chunks(t):
    b, s = t.shape[:2]
    return jnp.moveaxis(t.reshape(b, s // CHUNK, CHUNK, *t.shape[2:]), 1, 0)

def _layernorm(x, g, b):
    xf = x.astype(jnp.float32)
    mu = xf.mean(-1, keepdims=True)
    var = jnp.square(xf - mu).mean(-1, keepdims=True)
    return ((xf - mu) * lax.rsqrt(var + LN_EPS) * g.astype(jnp.float32) + b.astype(jnp.float32)).astype(x.dtype)

def _head_norm(y, n_groups, g, center):
    b, s, w = y.shape
    yf = y.astype(jnp.float32).reshape(b, s, n_groups, w // n_groups)
    if center:
        yf = yf - yf.mean(-1, keepdims=True)
    yf = yf * lax.rsqrt(jnp.square(yf).mean(-1, keepdims=True) + NORM_EPS)
    return yf.reshape(b, s, w) * g.astype(jnp.float32)

def _causal_conv(u, w, bias):
    ch = u.shape[-1]
    out = lax.conv_general_dilated(u, w[:, None, :].astype(u.dtype), window_strides=(1,),
                                   padding=[(CONV_K - 1, 0)], dimension_numbers=('NWC', 'WIO', 'NWC'),
                                   feature_group_count=ch)
    return out + bias

def _rotary(t, pos):
    d = t.shape[-1]
    inv_freq = ROPE_BASE ** (-jnp.arange(0, d, 2, dtype=jnp.float32) / d)
    ang = pos.astype(jnp.float32)[:, None, :, None] * inv_freq
    cos, sin = jnp.cos(ang), jnp.sin(ang)
    t1, t2 = t[..., 0::2], t[..., 1::2]
    return jnp.stack([t1 * cos - t2 * sin, t1 * sin + t2 * cos], axis=-1).reshape(t.shape)

def _retention(q, k, v):
    b, h, s, dk = q.shape
    dv = v.shape[-1]
    log_g = jnp.log(1.0 - 2.0 ** (-5.0 - jnp.arange(h, dtype=jnp.float32)))
    idx = jnp.arange(CHUNK, dtype=jnp.float32)
    diff = idx[:, None] - idx[None, :]
    mask = diff >= 0
    decay_intra = jnp.where(mask, jnp.exp(log_g[:, None, None] * jnp.where(mask, diff, 0.0)), 0.0)
    q_decay = jnp.exp(log_g[:, None] * (idx + 1.0))[..., None]
    k_decay = jnp.exp(log_g[:, None] * (CHUNK - 1.0 - idx))[..., None]
    chunk_decay = jnp.exp(log_g * CHUNK)[:, None, None]

    def step(state, inp):
        qi, ki, vi = inp
        scores = jnp.einsum('bhtd,bhsd->bhts', qi, ki) * decay_intra
        y = jnp.einsum('bhts,bhsv->bhtv', scores, vi) + jnp.einsum('bhtd,bhdv->bhtv', qi * q_decay, state)
        state = chunk_decay * state + jnp.einsum('bhsd,bhsv->bhdv', ki * k_decay, vi)
        return state, y

    state0 = jnp.zeros((b, h, dk, dv), jnp.float32)
    _, y = lax.scan(step, state0, (_chunks(q), _chunks(k), _chunks(v)))
    return _unchunk(y)

def _mlstm(q, k, v, i_pre, logf):
    b, h, s, dk = q.shape
    dv = v.shape[-1]
    causal = jnp.tril(jnp.ones((CHUNK, CHUNK), bool))

    def step(carry, inp):
        c_st, n_st, m_st = carry
        qi, ki, vi, ii, fi = inp
        bcum = jnp.cumsum(fi, axis=-1)
        a = bcum + m_st[..., None]
        d = jnp.where(causal, bcum[..., :, None] - bcum[..., None, :] + ii[..., None, :], -jnp.inf)
        m_t = jnp.maximum(a, d.max(-1))
        w_inter = jnp.exp(a - m_t)
        qk = jnp.einsum('bhtd,bhsd->bhts', qi, ki) * jnp.exp(d - m_t[..., None])
        num = jnp.einsum('bhts,bhsv->bhtv', qk, vi) + w_inter[..., None] * jnp.einsum('bhtd,bhdv->bhtv', qi, c_st)
        den = qk.sum(-1) + w_inter * jnp.einsum('bhtd,bhd->bht', qi, n_st)
        h_t = num / jnp.maximum(jnp.abs(den), jnp.exp(-m_t))[..., None]
        b_tot = bcum[..., -1]
        log_ws = b_tot[..., None] - bcum + ii
        m_new = jnp.maximum(b_tot + m_st, log_ws.max(-1))
        ks = ki * jnp.exp(log_ws - m_new[..., None])[..., None]
        decay = jnp.exp(b_tot + m_st - m_new)
        c_new = decay[..., None, None] * c_st + jnp.einsum('bhsd,bhsv->bhdv', ks, vi)
        n_new = decay[..., None] * n_st + ks.sum(-2)
        return (c_new, n_new, m_new), h_t

    carry0 = (jnp.zeros((b, h, dk, dv), jnp.float32), jnp.zeros((b, h, dk), jnp.float32),
              jnp.zeros((b, h), jnp.float32))
    _, y = lax.scan(step, carry0, (_chunks(q), _chunks(k), _chunks(v), _chunks(i_pre), _chunks(logf)))
    return _unchunk(y)

def _gla(q, k, v, log_alpha):
    b, h, s, dk = q.shape
    dv = v.shape[-1]
    causal = jnp.tril(jnp.ones((CHUNK, CHUNK), bool))[:, :, None]

    def step(state, inp):
        qi, ki, vi, gi = inp
        bcum = jnp.cumsum(gi, axis=-2)
        rel = jnp.where(causal, bcum[..., :, None, :] - bcum[..., None, :, :], -jnp.inf)
        scores = jnp.einsum('bhtd,bhsd,bhtsd->bhts', qi, ki, jnp.exp(rel))
        y = jnp.einsum('bhts,bhsv->bhtv', scores, vi) + jnp.einsum('bhtd,bhdv->bhtv', qi * jnp.exp(bcum), state)
        b_tot = bcum[..., -1:, :]
        state = jnp.exp(b_tot)[..., 0, :, None] * state + jnp.einsum('bhsd,bhsv->bhdv', ki * jnp.exp(b_tot - bcum), vi)
        return state, y

    state0 = jnp.zeros((b, h, dk, dv), jnp.float32)
    _, y = lax.scan(step, state0, (_chunks(q), _chunks(k), _chunks(v), _chunks(log_alpha)))
    return _unchunk(y)

def _ssd(xdt, log_a, bm, cm):
    b, s, g, r, p = xdt.shape
    n = bm.shape[-1]
    causal = jnp.tril(jnp.ones((CHUNK, CHUNK), bool))[None, :, :, None, None]

    def step(state, inp):
        xi, lai, bi, ci = inp
        cum = jnp.cumsum(lai, axis=1)
        seg = jnp.where(causal, cum[:, :, None] - cum[:, None, :], -jnp.inf)
        w = jnp.einsum('btgn,bsgn->btsg', ci, bi)[..., None] * jnp.exp(seg)
        y = jnp.einsum('btsgr,bsgrp->btgrp', w, xi) + jnp.exp(cum)[..., None] * jnp.einsum('btgn,bgrnp->btgrp', ci, state)
        last = cum[:, -1]
        xs = xi * jnp.exp(last[:, None] - cum)[..., None]
        state = jnp.exp(last)[..., None, None] * state + jnp.einsum('bsgn,bsgrp->bgrnp', bi, xs)
        return state, y

    state0 = jnp.zeros((b, g, r, n, p), jnp.float32)
    _, y = lax.scan(step, state0, (_seq_chunks(xdt), _seq_chunks(log_a), _seq_chunks(bm), _seq_chunks(cm)))
    return jnp.moveaxis(y, 0, 1).reshape(b, s, g * r, p)

def _mixer_ab(x, pos, w_in, ret_norm_g, ml_conv_w, ml_conv_b, ml_b_i, ml_b_f, ml_norm_g, w_out):
    f32 = jnp.float32
    proj = x @ w_in
    rq, rk, rv, rg, mq, mk, mv, mo, mi, mf = _split(proj, RET_SPLITS + ML_SPLITS)
    q = _rotary(_heads(rq, RET_H).astype(f32), pos)
    k = _rotary(_heads(rk, RET_H).astype(f32), pos) * RET_DK ** -0.5
    v = _heads(rv, RET_H).astype(f32)
    y_ret = _head_norm(_retention(q, k, v), RET_H, ret_norm_g, True) * jax.nn.silu(rg.astype(f32))
    qk = jax.nn.silu(_causal_conv(jnp.concatenate([mq, mk], axis=-1), ml_conv_w, ml_conv_b))
    cq, ck = jnp.split(qk, 2, axis=-1)
    q = _heads(cq, ML_H).astype(f32)
    k = _heads(ck, ML_H).astype(f32) * ML_DK ** -0.5
    v = _heads(mv, ML_H).astype(f32)
    i_pre = (mi + ml_b_i).astype(f32).transpose(0, 2, 1)
    logf = jax.nn.log_sigmoid((mf + ml_b_f).astype(f32)).transpose(0, 2, 1)
    h = _mlstm(q, k, v, i_pre, logf) * jax.nn.sigmoid(mo.astype(f32))
    y_ml = _head_norm(h, ML_H, ml_norm_g, True)
    y = jnp.concatenate([y_ret, y_ml], axis=-1).astype(x.dtype)
    return y @ w_out

def _mixer_cd(x, w_in, gla_w_alpha, gla_b_alpha, gla_norm_g, ssd_conv_w, ssd_conv_b, ssd_dt_bias, ssd_a_log,
              ssd_d, ssd_norm_g, w_out):
    f32 = jnp.float32
    b, s, _ = x.shape
    proj = x @ w_in
    gq, gk, gv, gr, ga, sz, sxbc, sdt = _split(proj, GLA_SPLITS + SSD_SPLITS)
    log_alpha = jax.nn.log_sigmoid((ga @ gla_w_alpha + gla_b_alpha).astype(f32)) / GLA_TAU
    q = _heads(gq, GLA_H).astype(f32) * GLA_DK ** -0.5
    k = _heads(gk, GLA_H).astype(f32)
    v = _heads(gv, GLA_H).astype(f32)
    y_gla = _head_norm(_gla(q, k, v, _heads(log_alpha, GLA_H)), GLA_H, gla_norm_g, False) * jax.nn.silu(gr.astype(f32))
    xbc = jax.nn.silu(_causal_conv(sxbc, ssd_conv_w, ssd_conv_b)).astype(f32)
    xs, bm, cm = _split(xbc, (SSD_DINNER, SSD_GROUPS * SSD_N, SSD_GROUPS * SSD_N))
    dt = jax.nn.softplus((sdt + ssd_dt_bias).astype(f32))
    a = -jnp.exp(ssd_a_log.astype(f32))
    xs_h = xs.reshape(b, s, SSD_H, SSD_HEADDIM)
    y = _ssd((xs_h * dt[..., None]).reshape(b, s, SSD_GROUPS, SSD_HPG, SSD_HEADDIM),
             (dt * a).reshape(b, s, SSD_GROUPS, SSD_HPG),
             bm.reshape(b, s, SSD_GROUPS, SSD_N), cm.reshape(b, s, SSD_GROUPS, SSD_N))
    y = (y + ssd_d.astype(f32)[:, None] * xs_h).reshape(b, s, SSD_DINNER) * jax.nn.silu(sz.astype(f32))
    y_ssd = _head_norm(y, SSD_GROUPS, ssd_norm_g, False)
    out = jnp.concatenate([y_gla, y_ssd], axis=-1).astype(x.dtype)
    return out @ w_out

def _moe(x, w_router, b_router, w_gate, w_up, w_down):
    b, s, d = x.shape
    xt = x.reshape(b * s, d)
    probs = jax.nn.softmax((xt @ w_router).astype(jnp.float32), axis=-1)
    sel = probs + b_router.astype(jnp.float32)
    grp_score = lax.top_k(sel.reshape(-1, N_EXPERT_GROUPS, EXPERTS_PER_GROUP), GROUP_SCORE_TOPK)[0].sum(-1)
    g_best = jnp.argmax(grp_score, axis=-1)
    in_group = (jnp.arange(N_EXPERTS) // EXPERTS_PER_GROUP)[None, :] == g_best[:, None]
    _, e_idx = lax.top_k(jnp.where(in_group, sel, -jnp.inf), TOP_K)
    gate = jnp.take_along_axis(probs, e_idx, axis=-1)
    gate = gate / gate.sum(-1, keepdims=True)
    combine = jnp.einsum('tk,tke->te', gate, jax.nn.one_hot(e_idx, N_EXPERTS, dtype=jnp.float32))
    y = jnp.zeros((b * s, d), jnp.float32)
    for e in range(N_EXPERTS):
        h = jax.nn.silu(xt @ w_gate[e]) * (xt @ w_up[e])
        y = y + combine[:, e:e + 1] * (h @ w_down[e]).astype(jnp.float32)
    return y.astype(x.dtype).reshape(b, s, d)

def setup_inputs(seed: int = 0) -> dict:
    key = jax.random.key(seed)
    ks = iter(jax.random.split(key, 40))
    f32 = jnp.float32

    def nrm(shape, scale):
        return scale * jax.random.normal(next(ks), shape, f32)

    def gain(shape):
        return 1.0 + nrm(shape, 0.02)

    x = jax.random.normal(next(ks), (BATCH, SEQ, D_MODEL), f32)
    offset = jax.random.randint(next(ks), (BATCH, 1), 0, 4096, dtype=jnp.int32)
    positions = (offset + jnp.arange(SEQ, dtype=jnp.int32)[None, :]).astype(jnp.int32)
    dt0 = jnp.exp(jax.random.uniform(next(ks), (N_ODD, SSD_H), f32, math.log(1e-3), math.log(1e-1)))
    return {
        'x': x,
        'positions': positions,
        'w_in_ab': nrm((N_EVEN, D_MODEL, P_AB), D_MODEL ** -0.5),
        'ret_norm_g': gain((N_EVEN, RET_H * RET_DV)),
        'ml_conv_w': nrm((N_EVEN, CONV_K, 2 * ML_H * ML_DK), CONV_K ** -0.5),
        'ml_conv_b': nrm((N_EVEN, 2 * ML_H * ML_DK), 0.02),
        'ml_b_i': nrm((N_EVEN, ML_H), 0.1),
        'ml_b_f': jnp.linspace(3.0, 6.0, ML_H, dtype=f32)[None, :] + nrm((N_EVEN, ML_H), 0.02),
        'ml_norm_g': gain((N_EVEN, ML_H * ML_DV)),
        'w_out_ab': nrm((N_EVEN, MIX_AB, D_MODEL), DEEPNORM_BETA * MIX_AB ** -0.5),
        'w_in_cd': nrm((N_ODD, D_MODEL, P_CD), D_MODEL ** -0.5),
        'gla_w_alpha': nrm((N_ODD, GLA_RANK, GLA_H * GLA_DK), GLA_RANK ** -0.5),
        'gla_b_alpha': nrm((N_ODD, GLA_H * GLA_DK), 0.02),
        'gla_norm_g': gain((N_ODD, GLA_H * GLA_DV)),
        'ssd_conv_w': nrm((N_ODD, CONV_K, SSD_DINNER + 2 * SSD_GROUPS * SSD_N), CONV_K ** -0.5),
        'ssd_conv_b': nrm((N_ODD, SSD_DINNER + 2 * SSD_GROUPS * SSD_N), 0.02),
        'ssd_dt_bias': dt0 + jnp.log(-jnp.expm1(-dt0)),
        'ssd_a_log': jnp.log(jax.random.uniform(next(ks), (N_ODD, SSD_H), f32, 1.0, 16.0)),
        'ssd_d': gain((N_ODD, SSD_H)),
        'ssd_norm_g': gain((N_ODD, SSD_DINNER)),
        'w_out_cd': nrm((N_ODD, MIX_CD, D_MODEL), DEEPNORM_BETA * MIX_CD ** -0.5),
        'w_router': nrm((D_MODEL, N_EXPERTS), D_MODEL ** -0.5),
        'b_router': nrm((N_EXPERTS,), 0.01),
        'moe_w_gate': nrm((DEPTH, N_EXPERTS, D_MODEL, D_FF), D_MODEL ** -0.5),
        'moe_w_up': nrm((DEPTH, N_EXPERTS, D_MODEL, D_FF), D_MODEL ** -0.5),
        'moe_w_down': nrm((DEPTH, N_EXPERTS, D_FF, D_MODEL), DEEPNORM_BETA * D_FF ** -0.5),
        'ln_mix_g': gain((DEPTH, D_MODEL)),
        'ln_mix_b': nrm((DEPTH, D_MODEL), 0.02),
        'ln_ffn_g': gain((DEPTH, D_MODEL)),
        'ln_ffn_b': nrm((DEPTH, D_MODEL), 0.02),
    }

def reference(x, positions, w_in_ab, ret_norm_g, ml_conv_w, ml_conv_b, ml_b_i, ml_b_f, ml_norm_g, w_out_ab,
              w_in_cd, gla_w_alpha, gla_b_alpha, gla_norm_g, ssd_conv_w, ssd_conv_b, ssd_dt_bias, ssd_a_log, ssd_d,
              ssd_norm_g, w_out_cd, w_router, b_router, moe_w_gate, moe_w_up, moe_w_down,
              ln_mix_g, ln_mix_b, ln_ffn_g, ln_ffn_b):
    h = x
    for layer in range(DEPTH):
        j = layer // 2
        if layer % 2 == 0:
            mix = _mixer_ab(h, positions, w_in_ab[j], ret_norm_g[j], ml_conv_w[j], ml_conv_b[j], ml_b_i[j],
                            ml_b_f[j], ml_norm_g[j], w_out_ab[j])
        else:
            mix = _mixer_cd(h, w_in_cd[j], gla_w_alpha[j], gla_b_alpha[j], gla_norm_g[j], ssd_conv_w[j],
                            ssd_conv_b[j], ssd_dt_bias[j], ssd_a_log[j], ssd_d[j], ssd_norm_g[j], w_out_cd[j])
        h = _layernorm(DEEPNORM_ALPHA * h + mix, ln_mix_g[layer], ln_mix_b[layer])
        ffn = _moe(h, w_router, b_router, moe_w_gate[layer], moe_w_up[layer], moe_w_down[layer])
        h = _layernorm(DEEPNORM_ALPHA * h + ffn, ln_ffn_g[layer], ln_ffn_b[layer])
    return h


_drawn_inputs = setup_inputs


def setup_inputs(seed=0):
    import zlib

    import numpy as np

    out = dict(_drawn_inputs(seed))
    spreads = {}
    factors = {'ret_norm_g': 3.87,
     'ml_b_i': 64.0,
     'gla_b_alpha': 8.0,
     'gla_norm_g': 9.27,
     'ssd_conv_b': 4.471,
     'ssd_d': 15.268,
     'ssd_norm_g': 10.633,
     'ml_conv_b': 3.304}
    for name, (base, spread) in spreads.items():
        noise = np.random.default_rng([zlib.crc32(name.encode()), seed]).standard_normal(out[name].shape)
        drawn = base * np.exp(spread * noise) if base else spread * noise
        out[name] = __import__('jax').numpy.asarray(drawn.astype(out[name].dtype))
    for name, factor in factors.items():
        out[name] = (out[name] * factor).astype(out[name].dtype)
    return out
```

```python
from contextlib import ExitStack

import numpy as np

import concourse.bass as bass
from concourse import mybir

F32 = mybir.dt.float32
I32 = mybir.dt.int32
ALU = mybir.AluOpType
ACT = mybir.ActivationFunctionType
AX = mybir.AxisListType

P = 128
SEQ = 256
TB = SEQ // P
D = 1024
KC = D // P
UNIT = 512
HEADS = 4
DK = 128
DV = 256
FF = 512
EXPERTS = 16
GROUPS = 4
PER_GROUP = EXPERTS // GROUPS
SSD_HEADS = 16
SSD_HD = 64
GLA_RANK = 16
MIX = 2048
CAUSAL = SEQ + P
LN_EPS = 1e-5
NORM_EPS = 1e-6
ALPHA = 4.0 ** 0.25
QK_SCALE = float(DK) ** -0.5
GLA_TAU = 16.0
GLA_BLOCK = 32
GLA_MID = 15
GLA_CAP = float(np.exp(35.0))
RING = 6
BLOCK = 64
PAIRS = EXPERTS // 2
ROWS = 2 * BLOCK
PASSES = SEQ // BLOCK
MOE_USES = (2, 2, 2, 2)
TWO_PI = 2.0 * np.pi
ROUND = 12582912.0
PI_A = 6.28125
PI_B = float(np.float32(np.round((TWO_PI - PI_A) * 2 ** 22) / 2 ** 22))
PI_C = float(TWO_PI - PI_A - PI_B)
PI_SAFE = 3.1415925
LOG_GAMMA = [float(np.log(1.0 - 2.0 ** (-5.0 - h))) for h in range(HEADS)]

C_ID, C_CAP, C_MASK, C_DIST = 0, 128, 128 + CAUSAL, 128 + 2 * CAUSAL
C_FREQ = 128 + 3 * CAUSAL
C_PRI = C_FREQ + 1
C_IOTA = C_PRI + EXPERTS
C_ALL = C_IOTA + BLOCK


def shape_constants():
    c = np.zeros((P, C_ALL), np.float32)
    c[:, C_ID:C_ID + P] = np.eye(P)
    s = np.arange(P)[:, None]
    dist = np.concatenate([np.arange(SEQ)[None, :] - s, np.arange(P)[None, :] - s], axis=1)
    c[:, C_CAP:C_CAP + CAUSAL] = np.where(dist >= 0, 0.0, -1e30)
    c[:, C_MASK:C_MASK + CAUSAL] = dist >= 0
    c[:, C_DIST:C_DIST + CAUSAL] = np.where(dist >= 0, dist, 1e5)
    half = np.arange(P) % (DK // 2)
    c[:, C_FREQ] = np.float32(10000.0) ** (-(2 * half).astype(np.float32) / np.float32(DK))
    c[:, C_PRI:C_PRI + EXPERTS] = EXPERTS - np.arange(EXPERTS)
    c[:, C_IOTA:C_IOTA + BLOCK] = 1 + np.arange(BLOCK)
    return c


AB_UNITS = [("w_in_ab", c) for c in
            [0, 512,
             1024, 1536, 2048, 2560,
             3072, 3584,
             4096, 4608, 5120, 5632]]
AB_TAIL = 6144
CD_UNITS = [("w_in_cd", c) for c in
            [0, 512,
             1024, 1536, 2048, 2560,
             4112, 4624, 5136, 5648,
             3088, 3600]]
CD_TAIL_A, CD_TAIL_DT = 3072, 6160
OUT_UNITS = 4
LAYER_UNITS = len(AB_UNITS) + OUT_UNITS
MOE_UNITS = 3 * EXPERTS
ROWS_AB = dict(norm=0, conv_w=16, conv_b=48, n=56)
ROWS_CD = dict(norm=0, conv_w=16, conv_b=80, b_alpha=96, n=100)


def build(nc, a, out, stop_after=None):
    with ExitStack() as ctx:
        def sb(name, shape, dt=F32):
            return ctx.enter_context(nc.sbuf_tensor(name, shape, dt))

        def sem(name):
            return ctx.enter_context(nc.semaphore(name))

        ctx.enter_context(nc.allow_non_contiguous_dma(reason="a few small parameter loads"))
        bank = [ctx.enter_context(nc.psum_tensor(f"bank{i}", [P, 512], F32)) for i in range(8)]

        ring = sb("ring", [P, RING, KC * UNIT])
        consts = sb("consts", [P, C_ALL])
        h = sb("h", [P, TB, D])
        hT = sb("hT", [P, KC, SEQ])
        feat = sb("feat", [P, 24, SEQ])
        tok = sb("tok", [P, 4, TB, D])
        yT = sb("yT", [P, MIX // P, SEQ])
        rows_ab = sb("rows_ab", [ROWS_AB["n"], P])
        rows_cd = sb("rows_cd", [ROWS_CD["n"], P])
        cols_ab = sb("cols_ab", [P, ROWS_AB["n"]])
        cols_cd = sb("cols_cd", [P, ROWS_CD["n"]])
        tail_ab = sb("tail_ab", [P, KC, 2 * HEADS])
        tail_a = sb("tail_a", [P, KC, GLA_RANK])
        tail_dt = sb("tail_dt", [P, KC, SSD_HEADS])
        w_alpha = sb("w_alpha", [GLA_RANK, HEADS * DK])
        w_router = sb("w_router", [P, KC, EXPERTS])
        b_router = sb("b_router", [P, TB, EXPERTS])
        ml_bias = sb("ml_bias", [HEADS, 2])
        ssd_par = sb("ssd_par", [SSD_HEADS, 2])
        ssd_d = sb("ssd_d", [P, SSD_HEADS])
        prob = sb("prob", [P, 2, CAUSAL])
        gate_row = sb("gate_row", [16, 5, SEQ])
        ones_row = sb("ones_row", [16, SEQ])
        ones_col = sb("ones_col", [P, 1])
        gate_col = sb("gate_col", [P, 2, TB, 16])
        stat = sb("stat", [P, 8, 6])
        mv = sb("mv", [P, TB, 2])
        rstd = sb("rstd", [P, TB])
        rec = sb("rec", [P, TB])
        eps = sb("eps", [P, 2])
        route = sb("route", [P, 8, TB, EXPERTS])
        rsmall = sb("rsmall", [P, 6, TB, GROUPS])
        rank = sb("rank", [P, TB, EXPERTS])
        load_f = sb("load_f", [P, 1])
        load_i = sb("load_i", [P, 1], I32)
        zero_row = sb("zero_row", [1, P])

        ident = consts[:, C_ID:C_ID + P]
        cap = consts[:, C_CAP:C_CAP + CAUSAL]
        cmask = consts[:, C_MASK:C_MASK + CAUSAL]
        dist = consts[:, C_DIST:C_DIST + CAUSAL]
        pri = consts[:, C_PRI:C_PRI + EXPERTS]
        trig = yT[:, 0:4, :].rearrange("p a t -> p (a t)").rearrange("p (a n) -> p a n", n=512)
        pos_i = yT[:, 4, :].bitcast(I32)
        pos_f = yT[:, 5, :]
        angle = yT[:, 6, :]
        turns = yT[:, 7:9, :]
        rot = yT[:, 10:14, :].rearrange("p a t -> p (a t)").rearrange("p (a n) -> p a n", n=512)
        bcum = yT[:, 8:12, :]
        gtmp = yT[:, 12:16, :]
        xdt = yT[:, 8:16, :].rearrange("p a t -> p (a t)").rearrange("p (b n) -> p b n", b=TB)
        dec = yT[:, 0:6, :].rearrange("p a t -> p (a t)").rearrange("p (r n) -> p r n", n=CAUSAL)
        mlexp = feat[:, 16:22, :].rearrange("p a t -> p (a t)").rearrange("p (r n) -> p r n", n=CAUSAL)
        xg = feat[:, 0:4, :].rearrange("p a t -> p (a t)").rearrange("p (k n) -> p k n", n=P)[:, :, 0:ROWS]
        sil = feat[:, 4:6, :].rearrange("p a t -> p (a t)")
        hid = feat[:, 6:8, :].rearrange("p a t -> p (a t)")
        hid_t = feat[:, 10:12, :].rearrange("p a t -> p (a t)").rearrange("p (k n) -> p k n", n=P)
        selw = feat[:, 8, :].rearrange("p (t n) -> p t n", n=P)[:, :, 0:ROWS]
        selw_t = feat[0:ROWS, 9, :]
        ye = feat[0:ROWS, 14:18, :].rearrange("p a t -> p (a t)")
        sel = tok[:, 1, :, :].rearrange("p t n -> p (t n)")[:, 0:TB * EXPERTS * BLOCK] \
            .rearrange("p (t e n) -> p t e n", t=TB, e=EXPERTS)
        lnp = tok[:, 2, :, :]

        ready = [sem(f"bank{i}_ready") for i in range(8)]
        stored = [sem(f"bank{i}_stored") for i in range(8)]
        ring_full = [sem(f"ring_full{i}") for i in range(RING)]
        out_used = sem("out_used")
        par_in = sem("par_in")
        x_in = sem("x_in")
        ln_in = sem("ln_in")
        dve_step = sem("dve_step")
        act_step = sem("act_step")
        out_done = sem("out_done")
        h_ready = sem("h_ready")
        trig_arg = sem("trig_arg")
        trig_done = sem("trig_done")
        dec_arg = sem("dec_arg")
        dec_done = sem("dec_done")
        dec_used = sem("dec_used")
        prob_ready = sem("prob_ready")
        rot_ready = sem("rot_ready")
        conv_first = sem("conv_first")
        conv_sum = sem("conv_sum")
        gate_a = sem("gate_a")
        gate_b = sem("gate_b")
        gate_ok = sem("gate_ok")
        var_ready = sem("var_ready")
        rstd_ready = sem("rstd_ready")
        y_done = sem("y_done")
        kscale = sem("kscale")
        kexp = sem("kexp")
        kused = sem("kused")
        r_exp = sem("r_exp")

        sel_ready = sem("sel_ready")
        rank_in = sem("rank_in")
        load_ready = sem("load_ready")

        class Pass:

            def __init__(self, tag, main=None):
                self.main = main is not None
                self.ready = ready if self.main else [sem(f"more{tag}_bank{i}_ready") for i in range(4)]
                self.stored = stored if self.main else [sem(f"more{tag}_bank{i}_stored") for i in range(4)]
                self.full = ring_full if self.main else [sem(f"more{tag}_full{i}") for i in range(RING)]
                self.selw = sem(f"selw{tag}_ready")
                self.sel = sem(f"sel{tag}_ready")
                self.base = main or {b: 0 for b in range(4)}
                self.next = None if self.main else sem(f"more{tag}_next")
                self.slots = None if self.main else sem(f"more{tag}_slots")

            def filled(self, eng, i, b, k):
                eng.wait_ge(self.ready[b], i * MOE_USES[b] + (self.base[b] + k + 1))

            def read(self, eng, i, b, k):
                eng.wait_ge(self.stored[b], i * MOE_USES[b] + (self.base[b] + k + 1))

            def claim(self, eng, i, b, k):
                if self.main or k:
                    eng.wait_ge(self.stored[b], i * MOE_USES[b] + (self.base[b] + k))

        uses = [0] * 8
        plan = {}

        def job(name, *banks):
            plan[name] = {b: uses[b] for b in banks}
            for b in banks:
                uses[b] += 1

        flip = [0]
        passes = {}

        def pair_job(name):
            job(name, *((0, 1), (2, 3))[flip[0] % 2])
            flip[0] += 1

        def single_job(name):
            job(name, (0, 2)[flip[0] % 2])
            flip[0] += 1

        def turn_jobs(tag):
            pair_job(tag + "0")
            pair_job(tag + "1")

        def moe_jobs(layer):
            job(f"router{layer}", 4)
            job(f"rank{layer}", 4)
            base = dict(enumerate(uses[0:4]))
            for b in range(4):
                uses[b] += PAIRS * MOE_USES[b]
            job(f"ffn{layer}", 4, 5, 6, 7)
            passes[layer] = Pass(layer, base), Pass(f"{layer}b")

        turn_jobs("x_turn")
        pair_job("params")
        for n in range(2):
            pair_job(f"ab{n}")
        single_job("gates")
        single_job("gate_cols")
        pair_job("gate_rows")
        for n in range(2, 6):
            pair_job(f"ab{n}")
        for hd in range(2):
            job(f"s_ret{hd}", 4 + hd % 2)
        pair_job("ab6")
        for hd in range(2):
            job(f"y_ret{hd}", 6 + hd % 2)
        for hd in range(2, 4):
            job(f"s_ret{hd}", 4 + hd % 2)
        pair_job("ab7")
        for hd in range(2, 4):
            job(f"y_ret{hd}", 6 + hd % 2)
        pair_job("ab8")
        pair_job("ab9")
        for hd in range(2):
            job(f"s_ml{hd}", 4 + hd % 2)
        pair_job("ab10")
        for hd in range(2):
            job(f"y_ml{hd}", 6 + hd % 2)
        for hd in range(2, 4):
            job(f"s_ml{hd}", 4 + hd % 2)
        pair_job("ab11")
        for hd in range(2, 4):
            job(f"y_ml{hd}", 6 + hd % 2)
        for n in range(4):
            pair_job(f"yturn0_{n}")
        job("mix0", 0, 1, 2, 3)
        turn_jobs("mix_turn0_")
        moe_jobs(0)
        turn_jobs("ffn_turn0_")

        for n in range(2):
            pair_job(f"cd{n}")
        pair_job("alpha_in")
        pair_job("alpha")
        single_job("dt_cols")
        for n in range(2, 6):
            pair_job(f"cd{n}")
        for hd in range(2):
            job(f"s_gla{hd}", 4 + hd % 2)
        pair_job("cd6")
        for hd in range(2):
            job(f"y_gla{hd}", 6 + hd % 2)
        for hd in range(2, 4):
            job(f"s_gla{hd}", 4 + hd % 2)
        pair_job("cd7")
        for hd in range(2, 4):
            job(f"y_gla{hd}", 6 + hd % 2)
        for n in range(8, 12):
            pair_job(f"cd{n}")
        for n in range(4):
            pair_job(f"xs_turn{n}")
        for g in range(GROUPS):
            pair_job(f"cum{g}")
            job(f"s_ssd{g}", 4 + g % 2)
            job(f"y_ssd{g}", 6 + g % 2)
        for n in range(4):
            pair_job(f"yturn1_{n}")
        job("mix1", 0, 1, 2, 3)
        turn_jobs("mix_turn1_")
        moe_jobs(1)

        def first_of(name):
            return min(plan[name])

        def wait_ready(eng, name, b):
            eng.wait_ge(ready[b], plan[name][b] + 1)

        def wait_stored(eng, name, b):
            eng.wait_ge(stored[b], plan[name][b] + 1)

        def unit_no(layer, n):
            return layer * (LAYER_UNITS + MOE_UNITS) + n

        tok_sets = {"ab2": (0, 0), "ab3": (0, 1), "ab4": (1, 0), "ab5": (1, 1), "ab8": (2, 0), "ab9": (2, 1),
                    "ab10": (3, 0), "ab11": (3, 1), "cd2": (0, 0), "cd3": (0, 1), "cd4": (1, 0), "cd5": (1, 1),
                    "cd10": (3, 0), "cd11": (3, 1)}

        def freed(n):
            layer, u = divmod(n, LAYER_UNITS + MOE_UNITS)
            if u < 12:
                name = ("ab", "cd")[layer] + str(u)
                b = max(plan[name])
                return ready[b], plan[name][b] + 1
            if u < LAYER_UNITS - 1:
                return out_used, layer * (OUT_UNITS - 1) + u - 11
            if u == LAYER_UNITS - 1:
                return ready[3], plan[f"mix{layer}"][3] + 1
            i, j = divmod(u - LAYER_UNITS, 6)
            b, k = (2 + j // 2, 0) if j < 4 else (3, 1)
            return ready[b], passes[layer][0].base[b] + MOE_USES[b] * i + k + 1

        par_list = [
            (consts[:, :], a["consts"]),
            (pos_i, a["positions"].to_broadcast([P, SEQ])),
            (rows_ab[0:8, :], a["ret_norm_g"].rearrange("o (k p) -> (o k) p", p=P)),
            (rows_ab[8:16, :], a["ml_norm_g"].rearrange("o (k p) -> (o k) p", p=P)),
            (rows_ab[16:48, :], a["ml_conv_w"].rearrange("o t (k p) -> (o t k) p", p=P)),
            (rows_ab[48:56, :], a["ml_conv_b"].rearrange("o (k p) -> (o k) p", p=P)),
            (rows_cd[0:8, :], a["gla_norm_g"].rearrange("o (k p) -> (o k) p", p=P)),
            (rows_cd[8:16, :], a["ssd_norm_g"].rearrange("o (k p) -> (o k) p", p=P)),
            (rows_cd[16:80, :], a["ssd_conv_w"].rearrange("o t (k p) -> (o t k) p", p=P)),
            (rows_cd[80:96, :], a["ssd_conv_b"].rearrange("o (k p) -> (o k) p", p=P)),
            (rows_cd[96:100, :], a["gla_b_alpha"].rearrange("o (k p) -> (o k) p", p=P)),
            (tail_ab[:, :, :], a["w_in_ab"][0, :, AB_TAIL:AB_TAIL + 2 * HEADS].rearrange("(k p) n -> p k n", p=P)),
            (tail_a[:, :, :], a["w_in_cd"][0, :, CD_TAIL_A:CD_TAIL_A + GLA_RANK].rearrange("(k p) n -> p k n", p=P)),
            (tail_dt[:, :, :],
             a["w_in_cd"][0, :, CD_TAIL_DT:CD_TAIL_DT + SSD_HEADS].rearrange("(k p) n -> p k n", p=P)),
            (w_alpha[:, :], a["gla_w_alpha"][0]),
            (w_router[:, :, :], a["w_router"].rearrange("(k p) n -> p k n", p=P)),
            (b_router[:, 0, :], a["b_router"].rearrange("(o n) -> o n", o=1).to_broadcast([P, EXPERTS])),
            (b_router[:, 1, :], a["b_router"].rearrange("(o n) -> o n", o=1).to_broadcast([P, EXPERTS])),
            (ml_bias[:, 0:1], a["ml_b_i"].rearrange("o n -> n o")),
            (ml_bias[:, 1:2], a["ml_b_f"].rearrange("o n -> n o")),
            (ssd_par[:, 0:1], a["ssd_dt_bias"].rearrange("o n -> n o")),
            (ssd_par[:, 1:2], a["ssd_a_log"].rearrange("o n -> n o")),
            (ssd_d[:, :], a["ssd_d"].to_broadcast([P, SSD_HEADS])),
        ]
        PAR_ALL = 16 * len(par_list)

        block = ctx.enter_context(nc.Block())

        @block.sync
        def _(sp):
            for b in range(TB):
                sp.dma_start(h[:, b, :], a["x"][0, b * P:(b + 1) * P, :]).then_inc(x_in, 16)

            def stream(n, dst, src):
                if n >= RING:
                    sp.wait_ge(*freed(n - RING))
                sp.dma_start(dst, src).then_inc(ring_full[n % RING], 16)

            def slot(n, k):
                return ring[:, n % RING, :].rearrange("p (k n) -> p k n", k=k)

            for layer, (units, w_out) in enumerate(((AB_UNITS, "w_out_ab"), (CD_UNITS, "w_out_cd"))):
                for u, (name, c0) in enumerate(units):
                    n = unit_no(layer, u)
                    stream(n, slot(n, KC), a[name][0, :, c0:c0 + UNIT].rearrange("(k p) n -> p k n", p=P))
                wo = a[w_out][0].rearrange("(k p) n -> p k n", p=P)
                for u in range(OUT_UNITS):
                    n = unit_no(layer, len(units) + u)
                    stream(n, slot(n, 4), wo[:, 4 * u:4 * u + 4, :])
                n0 = unit_no(layer, LAYER_UNITS)
                gate = a["moe_w_gate"].rearrange("l e (k p) n -> l e p k n", p=P)
                up = a["moe_w_up"].rearrange("l e (k p) n -> l e p k n", p=P)
                down = a["moe_w_down"].rearrange("l e (k p) n -> l e p k n", p=P)
                if stop_after == f"mix{layer}":
                    break
                pair = ((gate, 0, KC), (gate, 1, KC), (up, 0, KC), (up, 1, KC), (down, 0, FF // P),
                        (down, 1, FF // P))
                for j, (src, e, k) in enumerate(pair):
                    stream(n0 + j, slot(n0 + j, k), src[layer, e])
                with sp.Fori(1, PAIRS) as i:
                    for j, (src, e, k) in enumerate(pair):
                        n = n0 + j
                        done, count = freed(n)
                        sp.wait_ge(done, i * MOE_USES[3] + (count - MOE_USES[3]))
                        sp.dma_start(slot(n, k), src[layer, i * 2 + e]).then_inc(ring_full[n % RING], 16)
                sp.wait_ge(load_ready, layer + 1)
                load = sp.value_load(load_i[0:1, 0:1], min_val=0, max_val=SEQ)
                with sp.If(load > BLOCK):
                    for j in range(6):
                        sp.wait_ge(*freed(n0 + 6 * (PAIRS - 1) + j))
                    more = passes[layer][1]
                    with sp.Fori(0, PASSES - 1) as p:
                        with sp.Fori(0, PAIRS) as i:
                            sp.wait_ge(more.slots, p * PAIRS + i + 1)
                            for j, (src, e, k) in enumerate(pair):
                                n = n0 + j
                                sp.dma_start(slot(n, k), src[layer, i * 2 + e]).then_inc(more.full[n % RING], 16)
                    sp.wait_ge(more.slots, (PASSES - 1) * PAIRS + 1)
                if stop_after == f"moe{layer}":
                    break
            last = {"mix0": 1, "moe0": 2, "mix1": 3}.get(stop_after, 4)
            for b in range(TB):
                sp.wait_ge(h_ready, TB * (last - 1) + b + 1)
                sp.dma_start(out[0, b * P:(b + 1) * P, :], h[:, b, :]).then_inc(out_done, 16)
            sp.wait_ge(out_done, 16 * TB)

        @block.gpsimd
        def _(pool):
            for dst, src in par_list:
                pool.dma_start(dst, src).then_inc(par_in, 16)
            lns = [("ln_mix_g", "ln_mix_b", 0), ("ln_ffn_g", "ln_ffn_b", 0),
                   ("ln_mix_g", "ln_mix_b", 1), ("ln_ffn_g", "ln_ffn_b", 1)]
            for n, (g, b, l) in enumerate(lns):
                if n % 2:
                    pool.wait_ge(h_ready, TB * n)
                else:
                    pool.wait_ge(y_done, (8, 0, 12)[n])
                pool.dma_start(lnp[:, 0, :], a[g][l:l + 1, :].to_broadcast([P, D])).then_inc(ln_in, 16)
                pool.dma_start(lnp[:, 1, :], a[b][l:l + 1, :].to_broadcast([P, D])).then_inc(ln_in, 16)
                if {"mix0": 1, "moe0": 2, "mix1": 3}.get(stop_after, 4) == n + 1:
                    break

        @block.tensor
        def _(pe):
            def claim(name, b):
                if plan[name][b]:
                    pe.wait_ge(stored[b], plan[name][b])

            def mm(o, l, r, start=True, stop=True):
                return nc.tensor.matmul(o, l, r, start=start, stop=stop)

            def turn_h(tag):
                for j in range(2):
                    for q, b in enumerate(plan[f"{tag}{j}"]):
                        claim(f"{tag}{j}", b)
                        k0 = 4 * j + 2 * q
                        for k in range(2):
                            for t in range(TB):
                                last = nc.tensor.transpose(bank[b][:, k * SEQ + t * P:k * SEQ + (t + 1) * P],
                                                           h[:, t, (k0 + k) * P:(k0 + k + 1) * P], ident)
                        last.then_inc(ready[b], 1)

            def wait_hT(tag):
                for j in range(2):
                    for b in plan[f"{tag}{j}"]:
                        wait_stored(pe, f"{tag}{j}", b)

            def unit_in(n):
                pe.wait_ge(ring_full[n % RING], 16 * (n // RING + 1))

            def feature_unit(name, n, columns):
                unit_in(n)
                w = ring[:, n % RING, :].rearrange("p (k n) -> p k n", k=KC)
                for q, b in enumerate(plan[name]):
                    claim(name, b)
                    for m in (2 * q, 2 * q + 1):
                        for k in range(KC):
                            last = mm(bank[b][:, (m % 2) * SEQ:(m % 2 + 1) * SEQ], columns(w, k, m), hT[:, k, :],
                                      k == 0, k == KC - 1)
                    last.then_inc(ready[b], 1)

            def token_unit(name, n):
                unit_in(n)
                w = ring[:, n % RING, :].rearrange("p (k n) -> p k n", k=KC)
                for t, b in enumerate(plan[name]):
                    claim(name, b)
                    for k in range(KC):
                        last = mm(bank[b][:, :], hT[:, k, t * P:(t + 1) * P], w[:, k, :], k == 0, k == KC - 1)
                    last.then_inc(ready[b], 1)

            plain = lambda w, k, m: w[:, k, m * P:(m + 1) * P]
            pairs = lambda w, k, m: w[:, k, (m // 2) * SEQ + m % 2:(m // 2 + 1) * SEQ:2]

            def weights_out(layer, u):
                n = unit_no(layer, 12 + u)
                unit_in(n)
                w = ring[:, n % RING, :].rearrange("p (k n) -> p k n", k=4)
                for k in range(4):
                    for t in range(TB):
                        for half in range(2):
                            b = 2 * t + half
                            if u == 0 and k == 0:
                                claim(f"mix{layer}", b)
                            last = mm(bank[b][:, :], yT[:, 4 * u + k, t * P:(t + 1) * P],
                                      w[:, k, half * 512:(half + 1) * 512],
                                      u == 0 and k == 0, u == OUT_UNITS - 1 and k == 3)
                            if u == OUT_UNITS - 1 and k == 3:
                                last.then_inc(ready[b], 1)
                if u < OUT_UNITS - 1:
                    last.then_inc(out_used, 1)

            def y_turn(layer, n):
                name = f"yturn{layer}_{n}"
                if layer and n < 2:
                    wait_stored(pe, "y_gla3", first_of("y_gla3"))
                else:
                    pe.wait_ge(y_done, 12 if layer else 4 if n < 2 else 8)
                src = tok[:, 1 if n < 2 else 3, :, :]
                for q, b in enumerate(plan[name]):
                    claim(name, b)
                    for k in range(2):
                        c = (4 * n + 2 * q + k) % 8
                        for t in range(TB):
                            last = nc.tensor.transpose(bank[b][:, k * SEQ + t * P:k * SEQ + (t + 1) * P],
                                                       src[:, t, c * P:(c + 1) * P], ident)
                    last.then_inc(ready[b], 1)

            def values(name, b, n_prob, v, start_cols=0, width=DV, n_heads=1, den=None, tell=True, slots=None):
                for t in range(TB):
                    for j in range(t + 1):
                        lhs = slots[:, t * P:(t + 1) * P] if j == 0 else slots[:, SEQ:SEQ + P]
                        last = mm(bank[b][:, t * DV + start_cols:t * DV + start_cols + width], lhs, v(j),
                                  j == 0, j == t)
                return last

            def score_group(b, kk, qq, parts, start=True, stop=True):
                for j in range(2):
                    last = mm(bank[b][:, j * SEQ:j * SEQ + SEQ - j * P], kk[parts, j * P:(j + 1) * P],
                              qq[parts, j * P:SEQ], start, stop)
                return last

            full = slice(0, P)

            pe.wait_ge(x_in, 16 * TB)
            pe.wait_ge(par_in, PAR_ALL)
            pe.wait_ge(dve_step, 3)
            turn_h("x_turn")
            for (src, n_rows), b in zip(((rows_ab, ROWS_AB["n"]), (rows_cd, ROWS_CD["n"])), plan["params"]):
                claim("params", b)
                nc.tensor.transpose(bank[b][:, 0:n_rows], src[:, :], consts[0:n_rows, C_ID:C_ID + n_rows]) \
                    .then_inc(ready[b], 1)
            wait_hT("x_turn")
            feature_unit("ab0", unit_no(0, 0), pairs)
            feature_unit("ab1", unit_no(0, 1), pairs)

            bs = list(plan["gates"])
            claim("gates", bs[0])
            for q in range(2):
                for k in range(KC):
                    last = mm(bank[bs[0]][0:HEADS, q * SEQ:(q + 1) * SEQ],
                              tail_ab[:, k, q * HEADS:(q + 1) * HEADS], hT[:, k, :], k == 0, k == KC - 1)
            last.then_inc(ready[bs[0]], 1)

            def gate_turns():
                b0 = first_of("gate_cols")
                claim("gate_cols", b0)
                pe.wait_ge(gate_ok, 1)
                for q, row in enumerate((2, 4)):
                    for t in range(TB):
                        last = nc.tensor.transpose(bank[b0][:, (q * TB + t) * 16:(q * TB + t) * 16 + HEADS],
                                                   gate_row[0:HEADS, row, t * P:(t + 1) * P],
                                                   consts[0:HEADS, C_ID:C_ID + HEADS])
                last.then_inc(ready[b0], 1)
                for q, b in enumerate(plan["gate_rows"]):
                    claim("gate_rows", b)
                    for hd in (2 * q, 2 * q + 1):
                        last = mm(bank[b][:, (hd % 2) * SEQ:(hd % 2 + 1) * SEQ],
                                  consts[0:HEADS, C_ID + hd:C_ID + hd + 1].to_broadcast([HEADS, P]),
                                  gate_row[0:HEADS, 3, :])
                    last.then_inc(ready[b], 1)

            gate_turns()
            for u in range(2, 6):
                token_unit(f"ab{u}", unit_no(0, u))

            def s_ret(hd):
                b = first_of(f"s_ret{hd}")
                claim(f"s_ret{hd}", b)
                pe.wait_ge(rot_ready, 4)
                hp, part = hd // 2, slice(64 * (hd % 2), 64 * (hd % 2) + 64)
                for j in range(2):
                    for c in range(2):
                        last = mm(bank[b][:, j * SEQ:j * SEQ + SEQ - j * P],
                                  feat[part, 4 + 2 * hp + c, j * P:(j + 1) * P],
                                  feat[part, 2 * hp + c, j * P:SEQ], c == 0, c == 1)
                last.then_inc(ready[b], 1)

            def y_ret(hd):
                b = first_of(f"y_ret{hd}")
                claim(f"y_ret{hd}", b)
                wait_stored(pe, f"s_ret{hd}", first_of(f"s_ret{hd}"))
                if hd == 0:
                    for u in (2, 3):
                        for bb in plan[f"ab{u}"]:
                            wait_stored(pe, f"ab{u}", bb)
                values("", b, 0, lambda j: tok[:, 0, j, hd * DV:(hd + 1) * DV],
                       slots=prob[:, hd % 2, :]).then_inc(ready[b], 1)

            def s_ml(hd):
                b = first_of(f"s_ml{hd}")
                claim(f"s_ml{hd}", b)
                if hd == 0:
                    for u in (6, 7):
                        for bb in plan[f"ab{u}"]:
                            wait_stored(pe, f"ab{u}", bb)
                score_group(b, feat[:, 12 + hd, :], feat[:, 8 + hd, :], full).then_inc(ready[b], 1)

            def y_ml(hd):
                b, bd = first_of(f"y_ml{hd}"), first_of(f"s_ml{hd}")
                claim(f"y_ml{hd}", b)
                pe.wait_ge(prob_ready, hd + 1)
                if hd == 0:
                    for u in (8, 9):
                        for bb in plan[f"ab{u}"]:
                            wait_stored(pe, f"ab{u}", bb)
                slots = prob[:, hd % 2, :]
                for t in range(TB):
                    for j in range(t + 1):
                        mm(bank[bd][:, 400 + t:401 + t],
                           slots[:, t * P:(t + 1) * P] if j == 0 else slots[:, SEQ:SEQ + P], ones_col[:, :],
                           j == 0, j == t)
                values("", b, 0, lambda j: tok[:, 2, j, hd * DV:(hd + 1) * DV], slots=slots) \
                    .then_inc(ready[b], 1)

            s_ret(0)
            s_ret(1)
            feature_unit("ab6", unit_no(0, 6), plain)
            y_ret(0)
            y_ret(1)
            s_ret(2)
            s_ret(3)
            feature_unit("ab7", unit_no(0, 7), plain)
            y_ret(2)
            y_ret(3)
            for u in (8, 9):
                token_unit(f"ab{u}", unit_no(0, u))
            s_ml(0)
            s_ml(1)
            token_unit("ab10", unit_no(0, 10))
            y_ml(0)
            y_ml(1)
            s_ml(2)
            s_ml(3)
            token_unit("ab11", unit_no(0, 11))
            y_ml(2)
            y_ml(3)

            def project_out(layer):
                for n in range(4):
                    y_turn(layer, n)
                for u in range(OUT_UNITS):
                    if u == 0:
                        for n in range(4):
                            for b in plan[f"yturn{layer}_{n}"]:
                                wait_stored(pe, f"yturn{layer}_{n}", b)
                    weights_out(layer, u)

            project_out(0)

            def router(layer):
                b = 4
                claim(f"router{layer}", b)
                for t in range(TB):
                    for k in range(KC):
                        last = mm(bank[b][:, t * EXPERTS:(t + 1) * EXPERTS], hT[:, k, t * P:(t + 1) * P],
                                  w_router[:, k, :], k == 0, k == KC - 1)
                last.then_inc(ready[b], 1)

            def experts(w, i, full_at, gathered):
                n0 = unit_no(0 if w in passes[0] else 1, LAYER_UNITS)

                def weights(j, k):
                    n = n0 + j
                    pe.wait_ge(w.full[n % RING], full_at(n))
                    return ring[:, n % RING, :].rearrange("p (k n) -> p k n", k=k)

                for q in range(2):
                    w.claim(pe, i, q, 0)
                    mm(bank[q][:, 0:1], ident, ones_col[:, 0:1])
                    for c in range(4):
                        for t in range(TB):
                            last = mm(bank[q][:, c * P:c * P + ROWS], h[:, t, (4 * q + c) * P:(4 * q + c + 1) * P],
                                      sel[:, t, bass.ds(gathered * 2, 2), :], t == 0, t == TB - 1)
                    last.then_inc(w.ready[q], 1)
                w.read(pe, i, 0, 0)
                w.read(pe, i, 1, 0)
                for part in range(2):
                    w.claim(pe, i, 2 + part, 0)
                    wt = [weights(2 * part + e, KC) for e in range(2)]
                    for k in range(KC):
                        for e in range(2):
                            last = mm(bank[2 + part][e * BLOCK:(e + 1) * BLOCK, :], xg[:, k, e * BLOCK:(e + 1) * BLOCK],
                                      wt[e][:, k, :], k == 0, k == KC - 1)
                    last.then_inc(w.ready[2 + part], 1)
                w.claim(pe, i, 1, 1)
                pe.wait_ge(w.selw, i + 1)
                for t in range(TB):
                    last = nc.tensor.transpose(bank[1][:, t * P:(t + 1) * P], selw[:, t, :], ident)
                last.then_inc(w.ready[1], 1)
                w.claim(pe, i, 0, 1)
                pe.wait_ge(w.stored[3], i * MOE_USES[3] + (w.base[3] + 1))
                for c in range(FF // P):
                    last = nc.tensor.transpose(bank[0][:, c * P:(c + 1) * P], hid[:, c * P:(c + 1) * P], ident)
                last.then_inc(w.ready[0], 1)
                w.read(pe, i, 0, 1)
                for q in range(2):
                    w.claim(pe, i, 2 + q, 1)
                    wt = [weights(4 + e, FF // P) for e in range(2)]
                    for k in range(FF // P):
                        for e in range(2):
                            last = mm(bank[2 + q][e * BLOCK:(e + 1) * BLOCK, :], hid_t[:, k, e * BLOCK:(e + 1) * BLOCK],
                                      wt[e][:, k, q * 512:(q + 1) * 512], k == 0, k == FF // P - 1)
                    last.then_inc(w.ready[2 + q], 1)
                w.read(pe, i, 1, 1)
                for q in range(2):
                    w.read(pe, i, 2 + q, 1)
                    for t in range(TB):
                        last = nc.tensor.matmul(bank[4 + 2 * t + q][:, :], selw_t[:, t * P:(t + 1) * P],
                                                ye[:, q * 512:(q + 1) * 512], start=False, stop=False,
                                                skip_group_check=True)
                if not w.main:
                    last.then_inc(w.slots, 1)

            def moe(layer):
                pe.wait_ge(h_ready, TB * 2 * layer + TB)
                turn_h(f"mix_turn{layer}_")
                wait_hT(f"mix_turn{layer}_")
                router(layer)
                claim(f"rank{layer}", 4)
                pe.wait_ge(rank_in, layer + 1)
                upto, all_ones = cmask[:, 0:P], cmask[:, P:2 * P]
                picks = route[:, 2, :, :]
                mm(bank[4][:, 0:EXPERTS], upto, picks[:, 0, :])
                mm(bank[4][:, EXPERTS:2 * EXPERTS], all_ones, picks[:, 0, :], True, False)
                mm(bank[4][:, EXPERTS:2 * EXPERTS], upto, picks[:, 1, :], False, True)
                mm(bank[4][:, 2 * EXPERTS:3 * EXPERTS], all_ones, picks[:, 0, :], True, False)
                mm(bank[4][:, 2 * EXPERTS:3 * EXPERTS], all_ones, picks[:, 1, :], False, True) \
                    .then_inc(ready[4], 1)
                pe.wait_ge(load_ready, layer + 1)
                load = pe.value_load(load_i[0:1, 0:1], min_val=0, max_val=SEQ)
                for b in range(4, 8):
                    claim(f"ffn{layer}", b)
                    nc.tensor.matmul(bank[b][:, :], zero_row[0:1, :], consts[0:1, 0:512], start=True, stop=False,
                                     skip_group_check=True)
                first, more = passes[layer]
                pe.wait_ge(first.sel, 1)
                with pe.Fori(0, PAIRS) as i:
                    experts(first, i, lambda n: i * 16 + 16 * (n // RING + 1), i)
                with pe.If(load > BLOCK):
                    nc.tensor.matmul(bank[4][:, :], zero_row[0:1, :], consts[0:1, 0:512], start=False, stop=False,
                                     skip_group_check=True).then_inc(more.slots, 1)
                    with pe.Fori(0, PASSES - 1) as p:
                        pe.wait_ge(more.sel, p + 1)
                        nc.tensor.matmul(bank[4][:, :], zero_row[0:1, :], consts[0:1, 0:512], start=False,
                                         stop=False, skip_group_check=True)
                        with pe.Fori(0, PAIRS) as i:
                            at = p * PAIRS + i
                            experts(more, at, lambda n: at * 16 + 16, i)
                for b in range(4, 8):
                    nc.tensor.matmul(bank[b][:, :], zero_row[0:1, :], consts[0:1, 0:512], start=False, stop=True,
                                     skip_group_check=True).then_inc(ready[b], 1)

            if stop_after == "mix0":
                return
            moe(0)
            if stop_after == "moe0":
                return

            pe.wait_ge(h_ready, 2 * TB)
            turn_h("ffn_turn0_")
            wait_hT("ffn_turn0_")
            for u in range(2):
                feature_unit(f"cd{u}", unit_no(1, u), plain)
            b0, b1 = plan["alpha_in"]
            claim("alpha_in", b0)
            claim("alpha_in", b1)
            for b, w in ((b0, tail_a), (b1, tail_dt)):
                for k in range(KC):
                    last = mm(bank[b][0:16, 0:SEQ], w[:, k, :], hT[:, k, :], k == 0, k == KC - 1)
                last.then_inc(ready[b], 1)
            wait_stored(pe, "alpha_in", b0)
            for q, b in enumerate(plan["alpha"]):
                claim("alpha", b)
                for hd in (2 * q, 2 * q + 1):
                    last = mm(bank[b][:, (hd % 2) * SEQ:(hd % 2 + 1) * SEQ], w_alpha[:, hd * DK:(hd + 1) * DK],
                              gate_row[0:16, 0, :])
                last.then_inc(ready[b], 1)
            b0 = first_of("dt_cols")
            claim("dt_cols", b0)
            pe.wait_ge(gate_ok, 2)
            for q, row in enumerate((2, 3)):
                for t in range(TB):
                    last = nc.tensor.transpose(bank[b0][:, (q * TB + t) * 16:(q * TB + t + 1) * 16],
                                               gate_row[0:16, row, t * P:(t + 1) * P],
                                               consts[0:16, C_ID:C_ID + 16])
            last.then_inc(ready[b0], 1)
            for u in range(2, 6):
                token_unit(f"cd{u}", unit_no(1, u))

            def s_gla(hd):
                b = first_of(f"s_gla{hd}")
                claim(f"s_gla{hd}", b)
                for i in range(SEQ // GLA_BLOCK):
                    pe.wait_ge(kscale, 8 * hd + i + 1)
                    cols = slice(i * GLA_BLOCK, (i + 1) * GLA_BLOCK)
                    kk = gtmp[:, i % 2, :]
                    for j in range(2 if i >= 4 else 1):
                        last = mm(bank[b][:, j * P + cols.start:j * P + cols.stop], kk[:, j * P:(j + 1) * P],
                                  feat[:, hd, cols])
                    if i < SEQ // GLA_BLOCK - 1:
                        last.then_inc(kused, 1)
                last.then_inc(ready[b], 1)

            def y_gla(hd):
                b = first_of(f"y_gla{hd}")
                claim(f"y_gla{hd}", b)
                wait_stored(pe, f"s_gla{hd}", first_of(f"s_gla{hd}"))
                if hd == 0:
                    for u in (2, 3):
                        for bb in plan[f"cd{u}"]:
                            wait_stored(pe, f"cd{u}", bb)
                values("", b, 0, lambda j: tok[:, 0, j, hd * DV:(hd + 1) * DV],
                       slots=prob[:, hd % 2, :]).then_inc(ready[b], 1)

            s_gla(0)
            s_gla(1)
            feature_unit("cd6", unit_no(1, 6), plain)
            y_gla(0)
            y_gla(1)
            s_gla(2)
            s_gla(3)
            feature_unit("cd7", unit_no(1, 7), plain)
            y_gla(2)
            y_gla(3)
            for u in (8, 9):
                feature_unit(f"cd{u}", unit_no(1, u), plain)
            for u in (10, 11):
                token_unit(f"cd{u}", unit_no(1, u))
            for u in range(6, 10):
                for bb in plan[f"cd{u}"]:
                    wait_stored(pe, f"cd{u}", bb)
            for n in range(4):
                for q, b in enumerate(plan[f"xs_turn{n}"]):
                    claim(f"xs_turn{n}", b)
                    t, c0 = n // 2, 4 * (n % 2) + 2 * q
                    for c in range(2):
                        last = nc.tensor.transpose(bank[b][:, c * P:(c + 1) * P],
                                                   feat[:, 8 + c0 + c, t * P:(t + 1) * P], ident)
                    last.then_inc(ready[b], 1)
            for g in range(GROUPS):
                for q, b in enumerate(plan[f"cum{g}"]):
                    claim(f"cum{g}", b)
                    for r in (2 * q, 2 * q + 1):
                        hd = 4 * g + r
                        last = mm(bank[b][:, (r % 2) * SEQ:(r % 2 + 1) * SEQ],
                                  consts[0:16, C_ID + hd:C_ID + hd + 1].to_broadcast([16, P]),
                                  gate_row[0:16, 3, :])
                    last.then_inc(ready[b], 1)
                b = first_of(f"s_ssd{g}")
                claim(f"s_ssd{g}", b)
                score_group(b, feat[:, 16 + g, :], feat[:, 20 + g, :], full).then_inc(ready[b], 1)
                b = first_of(f"y_ssd{g}")
                claim(f"y_ssd{g}", b)
                if g == 0:
                    for n in range(4):
                        for bb in plan[f"xs_turn{n}"]:
                            wait_stored(pe, f"xs_turn{n}", bb)
                for r in range(4):
                    hd = 4 * g + r
                    if r < 3:
                        pe.wait_ge(prob_ready, HEADS + 3 * g + r + 1)
                    else:
                        wait_stored(pe, f"s_ssd{g}", first_of(f"s_ssd{g}"))
                    last = values("", b, 0, lambda j: xdt[:, j, hd * SSD_HD:(hd + 1) * SSD_HD],
                                  start_cols=r * SSD_HD, width=SSD_HD, slots=prob[:, hd % 2, :])
                    if r < 3:
                        last.then_inc(kused, 1)
                last.then_inc(ready[b], 1)
            project_out(1)
            if stop_after == "mix1":
                return
            moe(1)

        @block.scalar
        def _(act):
            steps = [0]

            def step(ins):
                ins.then_inc(act_step, 1)
                steps[0] += 1

            def settle():
                act.wait_ge(act_step, steps[0])

            def fn(o, i, f, **kw):
                return nc.scalar.activation(o, i, f, **kw)

            def copy_turn(name, q, dst):
                b = list(plan[name])[q]
                wait_ready(act, name, b)
                nc.scalar.copy(dst, bank[b][:, :]).then_inc(stored[b], 1)

            def turn_h(tag):
                for j in range(2):
                    copy_turn(f"{tag}{j}", 1, hT[:, 4 * j + 2:4 * j + 4, :].rearrange("p k t -> p (k t)"))

            def token_unit(name, f):
                i, half = tok_sets[name]
                for t, b in enumerate(plan[name]):
                    wait_ready(act, name, b)
                    fn(tok[:, i, t, half * 512:(half + 1) * 512], bank[b][:, :], f).then_inc(stored[b], 1)

            def root(n, e, src):
                act.wait_ge(var_ready, n)
                step(fn(rstd[:, :], src, ACT.Ln, bias=eps[:, e:e + 1]))
                settle()
                fn(rstd[:, :], rstd[:, :], ACT.Exp, scale=-0.5).then_inc(rstd_ready, 1)

            def conv_unit(name, first, cols, w0, b0, tile0, n_done):
                for m in range(4):
                    b = list(plan[name])[m // 2]
                    wait_ready(act, name, b)
                    fn(feat[:, first + m, :], bank[b][:, (m % 2) * SEQ:(m % 2 + 1) * SEQ], ACT.Identity,
                       scale=cols[:, w0 + tile0 + m:w0 + tile0 + m + 1],
                       bias=cols[:, b0 + tile0 + m:b0 + tile0 + m + 1]).then_inc(conv_first, 1)
                    act.wait_ge(conv_sum, n_done + m + 1)
                    ins = fn(feat[:, first + m, :], feat[:, first + m, :], ACT.Silu)
                    if m % 2:
                        ins.then_inc(stored[b], 1)

            act.wait_ge(dve_step, 5)
            act.wait_ge(par_in, PAR_ALL)
            turn_h("x_turn")
            act.wait_ge(trig_arg, 1)
            fn(trig[:, 0, 0:SEQ], turns[:, 0, :], ACT.Sin).then_inc(trig_done, 1)
            fn(trig[:, 0, SEQ:512], turns[:, 1, :], ACT.Sin).then_inc(trig_done, 1)
            act.wait_ge(gate_a, 1)
            step(fn(gate_row[0:HEADS, 1, :], gate_row[0:HEADS, 1, :], ACT.Exp, scale=-1.0))
            settle()
            fn(gate_row[0:HEADS, 1, :], gate_row[0:HEADS, 1, :], ACT.Ln, bias=1.0).then_inc(gate_b, 1)
            act.wait_ge(gate_a, 2)
            fn(gate_row[0:HEADS, 4, :], gate_row[0:HEADS, 4, :], ACT.Exp, scale=-1.0).then_inc(gate_ok, 1)
            for u in (2, 3):
                token_unit(f"ab{u}", ACT.Copy)
            for u in (4, 5):
                token_unit(f"ab{u}", ACT.Silu)
            act.wait_ge(rot_ready, 4)
            for hd in range(HEADS):
                fn(dec[:, hd, :], dist, ACT.Exp, scale=LOG_GAMMA[hd]).then_inc(dec_done, 1)
            root(1, 1, mv[:, :, 1])
            root(2, 1, mv[:, :, 1])
            conv_unit("ab6", 8, cols_ab, ROWS_AB["conv_w"] + 24, ROWS_AB["conv_b"], 0, 0)
            root(3, 1, mv[:, :, 1])
            root(4, 1, mv[:, :, 1])
            conv_unit("ab7", 12, cols_ab, ROWS_AB["conv_w"] + 24, ROWS_AB["conv_b"], 4, 4)
            for u in (8, 9):
                token_unit(f"ab{u}", ACT.Copy)
            wait_stored(act, "s_ret3", first_of("s_ret3"))
            for b in plan["gate_rows"]:
                wait_stored(act, "gate_rows", b)
            for hd in range(HEADS):
                fn(dec[:, hd, :], mlexp[:, hd, :], ACT.Exp).then_inc(dec_done, 1)
            token_unit("ab10", ACT.Sigmoid)
            root(5, 1, mv[:, :, 1])
            root(6, 1, mv[:, :, 1])
            token_unit("ab11", ACT.Sigmoid)
            root(7, 1, mv[:, :, 1])
            root(8, 1, mv[:, :, 1])

            def y_turns(layer, cols):
                for n in range(4):
                    b = list(plan[f"yturn{layer}_{n}"])[1]
                    wait_ready(act, f"yturn{layer}_{n}", b)
                    for k in range(2):
                        c = 4 * n + 2 + k
                        ins = fn(yT[:, c, :], bank[b][:, k * SEQ:(k + 1) * SEQ], ACT.Copy, scale=cols[:, c:c + 1])
                        step(ins) if k == 0 else ins.then_inc(stored[b], 1)

            y_turns(0, cols_ab)
            root(9, 0, mv[:, :, 1])

            def moe(layer):
                turn_h(f"mix_turn{layer}_")
                wait_stored(act, f"router{layer}", 4)
                fn(route[:, 0, :, :], route[:, 0, :, :], ACT.Exp).then_inc(r_exp, 1)
                act.wait_ge(load_ready, layer + 1)
                load = act.value_load(load_i[0:1, 0:1], min_val=0, max_val=SEQ)
                first, more = passes[layer]

                def experts(w, i):
                    w.filled(act, i, 0, 0)
                    fn(xg[:, 0:4, :], bank[0][:, :].rearrange("p (k n) -> p k n", n=P)[:, :, 0:ROWS],
                       ACT.Copy).then_inc(w.stored[0], 1)
                    w.filled(act, i, 2, 0)
                    fn(sil, bank[2][:, :], ACT.Silu).then_inc(w.stored[2], 1)
                    w.filled(act, i, 0, 1)
                    fn(hid_t.rearrange("p k n -> p (k n)"), bank[0][:, :], ACT.Copy).then_inc(w.stored[0], 1)
                    w.filled(act, i, 2, 1)
                    fn(ye[:, 0:512], bank[2][:, :], ACT.Copy).then_inc(w.stored[2], 1)

                with act.Fori(0, PAIRS) as i:
                    experts(first, i)
                with act.If(load > BLOCK):
                    with act.Fori(0, PASSES - 1) as p:
                        with act.Fori(0, PAIRS) as i:
                            experts(more, p * PAIRS + i)
                root(10 + 10 * layer, 0, mv[:, :, 1])

            if stop_after == "mix0":
                return
            moe(0)
            if stop_after == "moe0":
                return
            turn_h("ffn_turn0_")

            act.wait_ge(gate_a, 3)
            step(fn(gate_row[0:16, 2, :], gate_row[0:16, 1, :], ACT.Exp, scale=-1.0))
            settle()
            step(fn(gate_row[0:16, 2, :], gate_row[0:16, 2, :], ACT.Ln, bias=1.0))
            fn(ssd_par[:, 1:2], ssd_par[:, 1:2], ACT.Exp).then_inc(gate_b, 1)
            act.wait_ge(gate_a, 4)
            flat = gtmp.rearrange("p k t -> p (k t)")
            step(fn(flat, flat, ACT.Exp, scale=-1.0))
            settle()
            fn(flat, flat, ACT.Ln, bias=1.0).then_inc(gate_b, 1)
            for u in (2, 3):
                token_unit(f"cd{u}", ACT.Copy)
            for u in (4, 5):
                token_unit(f"cd{u}", ACT.Silu)

            def gla_head(hd):
                act.wait_ge(dec_arg, hd + 1)
                fn(dec[:, hd, 0:SEQ], dec[:, hd, 0:SEQ], ACT.Exp, scale=1.0 / GLA_TAU).then_inc(dec_done, 1)
                for i in range(SEQ // GLA_BLOCK):
                    n = P if i < 4 else SEQ
                    k = 8 * hd + i
                    if k >= 2:
                        act.wait_ge(kscale, k - 1)
                    fn(gtmp[:, 2 + i % 2, 0:n], bcum[:, hd, 0:n], ACT.Exp, scale=-1.0 / GLA_TAU,
                       bias=gate_col[:, 0, :, :].rearrange("p a b -> p (a b)")[:, k:k + 1]).then_inc(kexp, 1)

            act.wait_ge(gate_a, 5)
            gla_head(0)
            gla_head(1)
            root(11, 1, mv[:, :, 1])
            root(12, 1, mv[:, :, 1])
            conv_unit("cd6", 8, cols_cd, ROWS_CD["conv_w"] + 48, ROWS_CD["conv_b"], 0, 8)
            gla_head(2)
            gla_head(3)
            root(13, 1, mv[:, :, 1])
            root(14, 1, mv[:, :, 1])
            conv_unit("cd7", 12, cols_cd, ROWS_CD["conv_w"] + 48, ROWS_CD["conv_b"], 4, 12)
            conv_unit("cd8", 16, cols_cd, ROWS_CD["conv_w"] + 48, ROWS_CD["conv_b"], 8, 16)
            conv_unit("cd9", 20, cols_cd, ROWS_CD["conv_w"] + 48, ROWS_CD["conv_b"], 12, 20)
            for u in (10, 11):
                token_unit(f"cd{u}", ACT.Silu)
            for g in range(GROUPS):
                for r in range(4):
                    if r % 2:
                        b = list(plan[f"cum{g}"])[r // 2]
                        wait_stored(act, f"cum{g}", b)
                    else:
                        act.wait_ge(dec_arg, HEADS + 2 * g + r // 2 + 1)
                    fn(dec[:, r, :], dec[:, r, :], ACT.Exp).then_inc(dec_done, 1)
                root(15 + g, 1, mv[:, :, 1])
            y_turns(1, cols_cd)
            root(19, 0, mv[:, :, 1])
            if stop_after == "mix1":
                return
            moe(1)

        @block.vector
        def _(dve):
            V = nc.vector
            steps = [0]
            roots = [0]
            lns = [0]

            def step(ins):
                ins.then_inc(dve_step, 1)
                steps[0] += 1

            def settle():
                dve.wait_ge(dve_step, steps[0])

            def link(ins):
                step(ins)
                settle()

            def turn_h(tag):
                for j in range(2):
                    name = f"{tag}{j}"
                    b = list(plan[name])[0]
                    wait_ready(dve, name, b)
                    V.tensor_copy(hT[:, 4 * j:4 * j + 2, :].rearrange("p k t -> p (k t)"), bank[b][:, :]) \
                        .then_inc(stored[b], 1)

            step(V.memset(ones_row[:, :], 1.0))
            step(V.memset(ones_col[:, :], 1.0))
            step(V.memset(gate_col[:, :, :, :], 0.0))
            step(V.memset(eps[:, 0:1], LN_EPS))
            step(V.memset(eps[:, 1:2], NORM_EPS))
            step(V.memset(zero_row[:, :], 0.0))
            dve.wait_ge(par_in, PAR_ALL)
            turn_h("x_turn")
            for (dst, n), b in zip(((cols_ab, ROWS_AB["n"]), (cols_cd, ROWS_CD["n"])), plan["params"]):
                wait_ready(dve, "params", b)
                V.tensor_copy(dst[:, :], bank[b][:, 0:n]).then_inc(stored[b], 1)
            link(V.tensor_copy(pos_f, pos_i))
            link(V.tensor_scalar(angle, pos_f, consts[:, C_FREQ:C_FREQ + 1], None, ALU.mult))
            for q, shift in enumerate((0.25, 0.0)):
                link(V.tensor_scalar(turns[:, q, :], angle, 1.0 / TWO_PI, shift, ALU.mult, ALU.add))
                link(V.tensor_scalar(turns[:, q, :], turns[:, q, :], ROUND, None, ALU.add))
                link(V.tensor_scalar(turns[:, q, :], turns[:, q, :], -ROUND, None, ALU.add))
                link(V.scalar_tensor_tensor(out=pos_f, in0=turns[:, q, :], scalar=-PI_A, in1=angle,
                                            op0=ALU.mult, op1=ALU.add))
                link(V.scalar_tensor_tensor(out=pos_f, in0=turns[:, q, :], scalar=-PI_B, in1=pos_f,
                                            op0=ALU.mult, op1=ALU.add))
                link(V.scalar_tensor_tensor(out=turns[:, q, :], in0=turns[:, q, :], scalar=-PI_C, in1=pos_f,
                                            op0=ALU.mult, op1=ALU.add))
                link(V.tensor_scalar(turns[:, q, :], turns[:, q, :], float(TWO_PI * shift), PI_SAFE, ALU.add,
                                     ALU.min))
                ins = V.tensor_scalar(turns[:, q, :], turns[:, q, :], -PI_SAFE, None, ALU.max)
                if q == 0:
                    link(ins)
                else:
                    ins.then_inc(trig_arg, 1)
            dve.wait_ge(trig_done, 2)
            step(V.tensor_scalar(trig[:, 1, 0:SEQ], trig[:, 0, SEQ:512], -1.0, None, ALU.mult))
            link(V.tensor_copy(trig[:, 1, SEQ:512], trig[:, 0, 0:SEQ]))

            def rotate(name, first):
                for q, b in enumerate(plan[name]):
                    wait_ready(dve, name, b)
                    even = bank[b][:, 0:SEQ].rearrange("p (o t) -> p o t", o=1).to_broadcast([P, 2, SEQ])
                    odd = bank[b][:, SEQ:512].rearrange("p (o t) -> p o t", o=1).to_broadcast([P, 2, SEQ])
                    two = lambda x: x.rearrange("p (c t) -> p c t", c=2)
                    if q or name == "ab1":
                        dve.wait_ge(rot_ready, q + 2 * (name == "ab1"))
                    step(V.tensor_tensor(two(rot[:, 0, :]), even, two(trig[:, 0, :]), ALU.mult))
                    V.tensor_tensor(two(rot[:, 1, :]), odd, two(trig[:, 1, :]), ALU.mult).then_inc(stored[b], 1)
                    settle()
                    wait_stored(dve, name, b)
                    V.tensor_tensor(feat[:, first + 2 * q:first + 2 * q + 2, :], two(rot[:, 0, :]),
                                    two(rot[:, 1, :]), ALU.add).then_inc(rot_ready, 1)

            rotate("ab0", 0)
            rotate("ab1", 4)

            b0 = first_of("gates")
            wait_ready(dve, "gates", b0)
            G = gate_row[0:HEADS, :, :]
            link(V.tensor_scalar(G[:, 0, :], bank[b0][0:HEADS, SEQ:512], ml_bias[:, 1:2], None, ALU.add))
            V.tensor_scalar(G[:, 2, :], bank[b0][0:HEADS, 0:SEQ], ml_bias[:, 0:1], None, ALU.add) \
                .then_inc(stored[b0], 1)
            V.scalar_tensor_tensor(out=G[:, 1, :], in0=G[:, 0, :], scalar=-1.0, in1=G[:, 0, :], op0=ALU.mult,
                                   op1=ALU.max).then_inc(gate_a, 1)
            dve.wait_ge(gate_b, 1)
            link(V.scalar_tensor_tensor(out=G[:, 0, :], in0=G[:, 0, :], scalar=0.0, in1=G[:, 1, :],
                                        op0=ALU.min, op1=ALU.subtract))
            link(V.tensor_tensor_scan(G[:, 1, :], ones_row[0:HEADS, :], G[:, 0, :], 0.0, ALU.mult, ALU.add))
            link(V.tensor_tensor(G[:, 2, :], G[:, 2, :], G[:, 1, :], ALU.subtract))
            link(V.tensor_tensor_scan(G[:, 3, :], ones_row[0:HEADS, :], G[:, 2, :], 0.0, ALU.mult, ALU.max))
            link(V.tensor_tensor(G[:, 4, :], G[:, 1, :], G[:, 3, :], ALU.add))
            V.tensor_scalar(G[:, 3, :], G[:, 3, :], -1.0, None, ALU.mult).then_inc(gate_a, 1)
            b0 = first_of("gate_cols")
            wait_ready(dve, "gate_cols", b0)
            V.tensor_copy(gate_col[:, :, :, 0:HEADS],
                          bank[b0][:, 0:64].rearrange("p (q t n) -> p q t n", q=2, t=TB)[:, :, :, 0:HEADS]) \
                .then_inc(stored[b0], 1)
            wait_stored(dve, "gate_cols", b0)

            def decay_args(name, heads, buf, n0):
                for q, b in enumerate(plan[name]):
                    wait_ready(dve, name, b)
                    for r in (2 * q, 2 * q + 1):
                        for j in range(2):
                            ins = V.scalar_tensor_tensor(
                                out=buf(r)[:, j * SEQ:j * SEQ + SEQ - j * P],
                                in0=bank[b][:, (r % 2) * SEQ + j * P:(r % 2 + 1) * SEQ],
                                scalar=heads(r, j), in1=cap[:, j * SEQ:j * SEQ + SEQ - j * P],
                                op0=ALU.add, op1=ALU.min)
                            if j == 0:
                                step(ins)
                            else:
                                ins.then_inc(stored[b] if r % 2 else dec_arg, 1)

            for q, b in enumerate(plan["gate_rows"]):
                wait_ready(dve, "gate_rows", b)
                for r in (2 * q, 2 * q + 1):
                    for j in range(2):
                        ins = (V.scalar_tensor_tensor(
                            out=mlexp[:, r, j * SEQ:j * SEQ + SEQ - j * P],
                            in0=bank[b][:, (r % 2) * SEQ + j * P:(r % 2 + 1) * SEQ],
                            scalar=gate_col[:, 0, j, r:r + 1], in1=cap[:, j * SEQ:j * SEQ + SEQ - j * P],
                            op0=ALU.add, op1=ALU.min))
                        step(ins) if not (r % 2 and j) else ins.then_inc(stored[b], 1)

            def head_stats(src):
                for t in range(TB):
                    step(V.bn_stats(stat[:, t, :], src(t)))
                settle()
                step(V.bn_aggr(mv[:, 0, :], stat[:, 0, :]))
                V.bn_aggr(mv[:, 1, :], stat[:, 1, :]).then_inc(var_ready, 1)

            def wait_root():
                roots[0] += 1
                dve.wait_ge(rstd_ready, roots[0])
                dve.wait_ge(var_ready, roots[0])

            def decayed(s_name, b, n_prob, scale, factor, n_dec):
                wait_ready(dve, s_name, b)
                dve.wait_ge(dec_done, n_dec) if n_dec else None
                return V.scalar_tensor_tensor(out=prob[:, n_prob % 2, :], in0=bank[b][:, 0:CAUSAL], scalar=scale,
                                              in1=factor, op0=ALU.mult, op1=ALU.mult)

            def p_ret(hd):
                b = first_of(f"s_ret{hd}")
                decayed(f"s_ret{hd}", b, hd, QK_SCALE, dec[:, hd, :], hd + 1).then_inc(stored[b], 1)

            def y_ret(hd):
                b = first_of(f"y_ret{hd}")
                wait_ready(dve, f"y_ret{hd}", b)
                head_stats(lambda t: bank[b][:, t * DV:(t + 1) * DV])
                wait_root()
                cols = slice(hd * DV, (hd + 1) * DV)
                for u in (4, 5):
                    for bb in plan[f"ab{u}"]:
                        wait_stored(dve, f"ab{u}", bb)
                for t in range(TB):
                    ins = V.scalar_tensor_tensor(out=tok[:, 1, t, cols], in0=bank[b][:, t * DV:(t + 1) * DV],
                                                 scalar=mv[:, t, 0:1], in1=tok[:, 1, t, cols],
                                                 op0=ALU.subtract, op1=ALU.mult)
                    ins.then_inc(stored[b], 1) if t else step(ins)
                wait_stored(dve, f"y_ret{hd}", b)
                for t in range(TB):
                    ins = V.tensor_scalar(tok[:, 1, t, cols], tok[:, 1, t, cols], rstd[:, t:t + 1], None, ALU.mult)
                    link(ins) if t == 0 else ins.then_inc(y_done, 1)
                dve.wait_ge(y_done, hd + 1)

            p_ret(0)
            p_ret(1)
            y_ret(0)
            y_ret(1)

            def taps(name, first, cols, w0, n_tiles, tile0, n_done):
                for m in range(4):
                    b = list(plan[name])[m // 2]
                    dve.wait_ge(conv_first, n_done + m + 1)
                    for back in (1, 2, 3):
                        o = feat[:, first + m, back:SEQ]
                        c = w0 + (3 - back) * n_tiles + tile0 + m
                        ins = V.scalar_tensor_tensor(
                            out=o, in0=bank[b][:, (m % 2) * SEQ:(m % 2 + 1) * SEQ - back],
                            scalar=cols[:, c:c + 1], in1=o, op0=ALU.mult, op1=ALU.add)
                        link(ins) if back < 3 else ins.then_inc(conv_sum, 1)

            taps("ab6", 8, cols_ab, ROWS_AB["conv_w"], 8, 0, 0)
            p_ret(2)
            p_ret(3)
            y_ret(2)
            y_ret(3)
            taps("ab7", 12, cols_ab, ROWS_AB["conv_w"], 8, 4, 4)


            def p_ml(hd):
                b = first_of(f"s_ml{hd}")
                decayed(f"s_ml{hd}", b, hd, QK_SCALE, dec[:, hd, :], 4 + hd + 1).then_inc(prob_ready, 1)

            def y_ml(hd):
                b, bd = first_of(f"y_ml{hd}"), first_of(f"s_ml{hd}")
                wait_ready(dve, f"y_ml{hd}", b)
                V.tensor_copy(rec[:, :], bank[bd][:, 400:402]).then_inc(stored[bd], 1)
                wait_stored(dve, f"s_ml{hd}", bd)
                link(V.scalar_tensor_tensor(out=rec[:, :], in0=rec[:, :], scalar=-1.0, in1=rec[:, :], op0=ALU.mult,
                                            op1=ALU.max))
                link(V.tensor_tensor(rec[:, :], rec[:, :], gate_col[:, 1, :, hd], ALU.max))
                link(V.reciprocal(rec[:, :], rec[:, :]))
                cols = slice(hd * DV, (hd + 1) * DV)
                for bb in plan["ab10" if hd < 2 else "ab11"]:
                    wait_stored(dve, "ab10" if hd < 2 else "ab11", bb)
                for t in range(TB):
                    ins = V.scalar_tensor_tensor(out=tok[:, 3, t, cols], in0=bank[b][:, t * DV:(t + 1) * DV],
                                                 scalar=rec[:, t:t + 1], in1=tok[:, 3, t, cols],
                                                 op0=ALU.mult, op1=ALU.mult)
                    ins.then_inc(stored[b], 1) if t else step(ins)
                wait_stored(dve, f"y_ml{hd}", b)
                head_stats(lambda t: tok[:, 3, t, cols])
                wait_root()
                for t in range(TB):
                    ins = V.tensor_scalar(tok[:, 3, t, cols], tok[:, 3, t, cols], mv[:, t, 0:1], rstd[:, t:t + 1],
                                          ALU.subtract, ALU.mult)
                    link(ins) if t == 0 else ins.then_inc(y_done, 1)
                dve.wait_ge(y_done, 4 + hd + 1)

            p_ml(0)
            p_ml(1)
            y_ml(0)
            y_ml(1)
            p_ml(2)
            p_ml(3)
            y_ml(2)
            y_ml(3)

            def y_turns(layer, cols):
                for n in range(4):
                    b = list(plan[f"yturn{layer}_{n}"])[0]
                    wait_ready(dve, f"yturn{layer}_{n}", b)
                    for k in range(2):
                        c = 4 * n + k
                        ins = V.tensor_scalar(yT[:, c, :], bank[b][:, k * SEQ:(k + 1) * SEQ], cols[:, c:c + 1], None,
                                              ALU.mult)
                        step(ins) if k == 0 else ins.then_inc(stored[b], 1)

            def layernorm(add, n_ready):
                for t in range(TB):
                    for half in range(2):
                        add(t, half)
                settle()
                for t in range(TB):
                    for half in range(2):
                        step(V.bn_stats(stat[:, 2 * t + half, :], h[:, t, half * 512:(half + 1) * 512]))
                settle()
                step(V.bn_aggr(mv[:, 0, :], stat[:, 0:2, :]))
                V.bn_aggr(mv[:, 1, :], stat[:, 2:4, :]).then_inc(var_ready, 1)
                wait_root()
                dve.wait_ge(ln_in, 32 * (n_ready // TB + 1))
                for t in range(TB):
                    step(V.tensor_scalar(h[:, t, :], h[:, t, :], mv[:, t, 0:1], rstd[:, t:t + 1], ALU.subtract,
                                         ALU.mult))
                settle()
                for t in range(TB):
                    step(V.tensor_tensor(h[:, t, :], h[:, t, :], lnp[:, 0, :], ALU.mult))
                settle()
                for t in range(TB):
                    V.tensor_tensor(h[:, t, :], h[:, t, :], lnp[:, 1, :], ALU.add).then_inc(h_ready, 1)

            def add_mix(layer):
                def add(t, half):
                    b = 2 * t + half
                    wait_ready(dve, f"mix{layer}", b)
                    V.scalar_tensor_tensor(out=h[:, t, half * 512:(half + 1) * 512],
                                           in0=h[:, t, half * 512:(half + 1) * 512], scalar=ALPHA,
                                           in1=bank[b][:, :], op0=ALU.mult, op1=ALU.add).then_inc(stored[b], 1)
                    wait_stored(dve, f"mix{layer}", b)
                return add

            y_turns(0, cols_ab)
            layernorm(add_mix(0), 0)

            def routing(layer):
                b = 4
                name = f"router{layer}"
                wait_ready(dve, name, b)
                R = route
                logits = bank[b][:, 0:TB * EXPERTS].rearrange("p (t e) -> p t e", t=TB)
                wide = lambda x: x.rearrange("p (t o) -> p t o", o=1).to_broadcast([P, TB, EXPERTS])
                mx, sm = rstd[:, :], rec[:, :]
                grp = lambda x: x.rearrange("p t (g e) -> p t g e", g=GROUPS)
                link(V.tensor_reduce(mx, logits, AX.X, ALU.max))
                V.tensor_tensor(R[:, 0, :, :], logits, wide(mx), ALU.subtract).then_inc(stored[b], 1)
                dve.wait_ge(r_exp, layer + 1)
                link(V.tensor_reduce(sm, R[:, 0, :, :], AX.X, ALU.add))
                link(V.reciprocal(sm, sm))
                link(V.tensor_tensor(R[:, 0, :, :], R[:, 0, :, :], wide(sm), ALU.mult))
                link(V.tensor_tensor(R[:, 1, :, :], R[:, 0, :, :], b_router[:, :, :], ALU.add))
                s = grp(R[:, 1, :, :])
                S = lambda i: rsmall[:, i, :, :]
                m = [s[:, :, :, i] for i in range(PER_GROUP)]
                link(V.tensor_tensor(S(0), m[0], m[1], ALU.max))
                link(V.tensor_tensor(S(1), m[0], m[1], ALU.min))
                link(V.tensor_tensor(S(2), m[2], m[3], ALU.max))
                link(V.tensor_tensor(S(3), m[2], m[3], ALU.min))
                link(V.tensor_tensor(S(4), S(0), S(2), ALU.max))
                link(V.tensor_tensor(S(5), S(0), S(2), ALU.min))
                link(V.tensor_tensor(S(1), S(1), S(3), ALU.max))
                link(V.tensor_tensor(S(1), S(1), S(5), ALU.max))
                link(V.tensor_tensor(S(4), S(4), S(1), ALU.add))
                narrow = lambda x: x.rearrange("p (t o) -> p t o", o=1).to_broadcast([P, TB, GROUPS])
                order4 = pri[:, EXPERTS - GROUPS:EXPERTS].rearrange("p (o e) -> p o e", o=1) \
                    .to_broadcast([P, TB, GROUPS])
                order16 = pri.rearrange("p (o e) -> p o e", o=1).to_broadcast([P, TB, EXPERTS])
                link(V.tensor_reduce(mx, S(4), AX.X, ALU.max))
                link(V.tensor_tensor(S(0), S(4), narrow(mx), ALU.is_equal))
                link(V.tensor_tensor(S(0), S(0), order4, ALU.mult))
                link(V.tensor_reduce(mx, S(0), AX.X, ALU.max))
                link(V.tensor_tensor(S(0), S(0), narrow(mx), ALU.is_equal))
                link(V.tensor_scalar(S(0), S(0), 1e30, -1e30, ALU.mult, ALU.add))
                for t in range(TB):
                    in_group = rsmall[:, 0, t, :].rearrange("p (g o) -> p g o", o=1) \
                        .to_broadcast([P, GROUPS, PER_GROUP])
                    link(V.tensor_tensor(R[:, 1, t, :].rearrange("p (g e) -> p g e", g=GROUPS),
                                         R[:, 1, t, :].rearrange("p (g e) -> p g e", g=GROUPS), in_group, ALU.add))
                for pick in (2, 3):
                    link(V.tensor_reduce(mx, R[:, 1, :, :], AX.X, ALU.max))
                    link(V.tensor_tensor(R[:, pick, :, :], R[:, 1, :, :], wide(mx), ALU.is_equal))
                    link(V.tensor_tensor(R[:, pick, :, :], R[:, pick, :, :], order16, ALU.mult))
                    link(V.tensor_reduce(mx, R[:, pick, :, :], AX.X, ALU.max))
                    link(V.tensor_tensor(R[:, pick, :, :], R[:, pick, :, :], wide(mx), ALU.is_equal))
                    if pick == 2:
                        link(V.scalar_tensor_tensor(out=R[:, 1, :, :], in0=R[:, pick, :, :], scalar=-2e30,
                                                    in1=R[:, 1, :, :], op0=ALU.mult, op1=ALU.add))
                V.tensor_tensor(R[:, 2, :, :], R[:, 2, :, :], R[:, 3, :, :], ALU.add).then_inc(rank_in, 1)
                dve.wait_ge(rank_in, layer + 1)
                link(V.tensor_tensor(R[:, 3, :, :], R[:, 2, :, :], R[:, 0, :, :], ALU.mult))
                link(V.tensor_reduce(sm, R[:, 3, :, :], AX.X, ALU.add))
                link(V.reciprocal(sm, sm))
                link(V.tensor_tensor(R[:, 4, :, :], R[:, 3, :, :], wide(sm), ALU.mult))

            def moe(layer):
                turn_h(f"mix_turn{layer}_")
                routing(layer)
                first, more = passes[layer]
                wait_ready(dve, f"rank{layer}", 4)
                counts = bank[4][:, 0:3 * EXPERTS].rearrange("p (t e) -> p t e", e=EXPERTS)
                step(V.tensor_tensor(rank[:, :, :], counts[:, 0:TB, :], route[:, 2, :, :], ALU.mult))
                V.tensor_reduce(load_f[:, :], counts[:, TB, :], AX.X, ALU.max).then_inc(stored[4], 1)
                wait_stored(dve, f"rank{layer}", 4)
                V.tensor_copy(load_i[:, :], load_f[:, :]).then_inc(load_ready, 1)
                n_lists = TB * EXPERTS
                places = consts[:, C_IOTA:C_IOTA + BLOCK]

                def pick(w):
                    V.tensor_tensor(sel.rearrange("p t e n -> p (t e) n"),
                                    places.rearrange("p (o n) -> p o n", o=1).to_broadcast([P, n_lists, BLOCK]),
                                    rank.rearrange("p t e -> p (t e)").rearrange("p (l o) -> p l o", o=1)
                                    .to_broadcast([P, n_lists, BLOCK]), ALU.is_equal).then_inc(w.sel, 1)

                pick(first)
                dve.wait_ge(load_ready, layer + 1)
                load = dve.value_load(load_i[0:1, 0:1], min_val=0, max_val=SEQ)

                def experts(w, i, e0):
                    for t in range(TB):
                        for e in range(2):
                            ins = V.tensor_scalar(selw[:, t, e * BLOCK:(e + 1) * BLOCK], places,
                                                  rank[:, t, bass.ds(e0 * 2 + e, 1)],
                                                  route[:, 4, t, bass.ds(e0 * 2 + e, 1)], ALU.is_equal, ALU.mult)
                    ins.then_inc(w.selw, 1)
                    w.filled(dve, i, 1, 0)
                    V.tensor_copy(xg[:, 4:8, :], bank[1][:, :].rearrange("p (k n) -> p k n", n=P)[:, :, 0:ROWS]) \
                        .then_inc(w.stored[1], 1)
                    w.read(dve, i, 2, 0)
                    w.filled(dve, i, 3, 0)
                    V.tensor_tensor(hid, sil, bank[3][:, :], ALU.mult).then_inc(w.stored[3], 1)
                    w.filled(dve, i, 1, 1)
                    V.tensor_copy(selw_t, bank[1][:, 0:SEQ]).then_inc(w.stored[1], 1)
                    w.filled(dve, i, 3, 1)
                    V.tensor_copy(ye[:, 512:1024], bank[3][:, :]).then_inc(w.stored[3], 1)

                with dve.Fori(0, PAIRS) as i:
                    experts(first, i, i)
                with dve.If(load > BLOCK):
                    with dve.Fori(0, PASSES - 1) as p:
                        V.tensor_scalar(rank[:, :, :], rank[:, :, :], float(BLOCK), None, ALU.subtract) \
                            .then_inc(more.next, 1)
                        dve.wait_ge(more.next, p + 1)
                        pick(more)
                        with dve.Fori(0, PAIRS) as i:
                            experts(more, p * PAIRS + i, i)

                def add(t, half):
                    b = 4 + 2 * t + half
                    wait_ready(dve, f"ffn{layer}", b)
                    V.scalar_tensor_tensor(out=h[:, t, half * 512:(half + 1) * 512],
                                           in0=h[:, t, half * 512:(half + 1) * 512], scalar=ALPHA,
                                           in1=bank[b][:, :], op0=ALU.mult, op1=ALU.add).then_inc(stored[b], 1)
                    wait_stored(dve, f"ffn{layer}", b)
                layernorm(add, 2 * TB * layer + TB)

            if stop_after == "mix0":
                return
            moe(0)
            if stop_after == "moe0":
                return
            turn_h("ffn_turn0_")

            for u, first in ((0, 0), (1, 4)):
                for q, b in enumerate(plan[f"cd{u}"]):
                    wait_ready(dve, f"cd{u}", b)
                    V.tensor_copy(feat[:, first + 2 * q:first + 2 * q + 2, :].rearrange("p k t -> p (k t)"),
                                  bank[b][:, :]).then_inc(stored[b], 1)
            b0, b1 = plan["alpha_in"]
            G = gate_row[0:16, :, :]
            wait_ready(dve, "alpha_in", b0)
            V.tensor_copy(G[:, 0, :], bank[b0][0:16, 0:SEQ]).then_inc(stored[b0], 1)
            wait_ready(dve, "alpha_in", b1)
            V.tensor_scalar(G[:, 4, :], bank[b1][0:16, 0:SEQ], ssd_par[:, 0:1], None, ALU.add) \
                .then_inc(stored[b1], 1)
            wait_stored(dve, "alpha_in", b1)
            V.scalar_tensor_tensor(out=G[:, 1, :], in0=G[:, 4, :], scalar=-1.0, in1=G[:, 4, :], op0=ALU.mult,
                                   op1=ALU.max).then_inc(gate_a, 1)
            dve.wait_ge(gate_b, 2)
            link(V.scalar_tensor_tensor(out=G[:, 2, :], in0=G[:, 4, :], scalar=0.0, in1=G[:, 2, :],
                                        op0=ALU.max, op1=ALU.add))
            link(V.tensor_scalar(G[:, 1, :], G[:, 2, :], ssd_par[:, 1:2], -1.0, ALU.mult, ALU.mult))
            V.tensor_tensor_scan(G[:, 3, :], ones_row[0:16, :], G[:, 1, :], 0.0, ALU.mult, ALU.add) \
                .then_inc(gate_ok, 1)
            for q, b in enumerate(plan["alpha"]):
                wait_ready(dve, "alpha", b)
                for hd in (2 * q, 2 * q + 1):
                    ins = V.tensor_scalar(bcum[:, hd, :], bank[b][:, (hd % 2) * SEQ:(hd % 2 + 1) * SEQ],
                                          cols_cd[:, ROWS_CD["b_alpha"] + hd:ROWS_CD["b_alpha"] + hd + 1], None,
                                          ALU.add)
                    ins.then_inc(stored[b], 1) if hd % 2 else step(ins)
                wait_stored(dve, "alpha", b)
            V.scalar_tensor_tensor(out=gtmp, in0=bcum, scalar=-1.0, in1=bcum, op0=ALU.mult, op1=ALU.max).then_inc(gate_a, 1)
            dve.wait_ge(gate_b, 3)
            link(V.scalar_tensor_tensor(out=gtmp, in0=bcum, scalar=0.0, in1=gtmp, op0=ALU.min, op1=ALU.subtract))
            link(V.memset(dec[:, 0, 0:SEQ], 1.0))
            for hd in range(HEADS):
                link(V.tensor_tensor_scan(bcum[:, hd, :], dec[:, 0, 0:SEQ], gtmp[:, hd, :], 0.0, ALU.mult, ALU.add))
            b0 = first_of("dt_cols")
            wait_ready(dve, "dt_cols", b0)
            link(V.tensor_copy(gate_col[:, 1, :, :], bank[b0][:, 0:32].rearrange("p (t n) -> p t n", t=TB)))
            V.tensor_scalar(route[:, 5, :, :], bank[b0][:, 32:64].rearrange("p (t n) -> p t n", t=TB), -1.0,
                            None, ALU.mult).then_inc(stored[b0], 1)
            refs = gate_col[:, 0, :, :].rearrange("p a b -> p (a b)").rearrange("p (h i) -> p h i", h=HEADS)
            V.tensor_scalar(refs, bcum[:, :, GLA_MID::GLA_BLOCK], 1.0 / GLA_TAU, None, ALU.mult) \
                .then_inc(gate_a, 1)
            dve.wait_ge(gate_a, 5)

            def gla_head(hd):
                blocks = lambda x: x.rearrange("p (i c) -> p i c", c=GLA_BLOCK)
                V.tensor_tensor(blocks(dec[:, hd, 0:SEQ]), blocks(bcum[:, hd, :]),
                                bcum[:, hd, GLA_MID::GLA_BLOCK].rearrange("p (i o) -> p i o", o=1)
                                .to_broadcast([P, SEQ // GLA_BLOCK, GLA_BLOCK]), ALU.subtract).then_inc(dec_arg, 1)
                dve.wait_ge(dec_done, 8 + hd + 1)
                link(V.scalar_tensor_tensor(out=feat[:, hd, :], in0=dec[:, hd, 0:SEQ], scalar=GLA_CAP,
                                            in1=feat[:, hd, :], op0=ALU.min, op1=ALU.mult))
                for i in range(SEQ // GLA_BLOCK):
                    n = P if i < 4 else SEQ
                    k = 8 * hd + i
                    dve.wait_ge(kexp, k + 1)
                    if i >= 2:
                        dve.wait_ge(kused, 7 * hd + i - 1)
                    elif hd:
                        dve.wait_ge(kused, 7 * hd)
                        wait_ready(dve, f"s_gla{hd - 1}", first_of(f"s_gla{hd - 1}"))
                    V.scalar_tensor_tensor(out=gtmp[:, i % 2, 0:n], in0=gtmp[:, 2 + i % 2, 0:n], scalar=GLA_CAP,
                                           in1=feat[:, 4 + hd, 0:n], op0=ALU.min, op1=ALU.mult) \
                        .then_inc(kscale, 1)

            def p_gla(hd):
                b = first_of(f"s_gla{hd}")
                decayed(f"s_gla{hd}", b, hd, QK_SCALE, cmask, 0).then_inc(stored[b], 1)

            def square_mean(src):
                for t in range(TB):
                    link(V.bn_stats(stat[:, t, :], src(t)))
                    link(V.bn_aggr(mv[:, t, :], stat[:, t, :]))
                link(V.tensor_tensor(mv[:, :, 0], mv[:, :, 0], mv[:, :, 0], ALU.mult))
                V.tensor_tensor(mv[:, :, 1], mv[:, :, 1], mv[:, :, 0], ALU.add).then_inc(var_ready, 1)

            def y_gla(hd):
                b = first_of(f"y_gla{hd}")
                wait_ready(dve, f"y_gla{hd}", b)
                square_mean(lambda t: bank[b][:, t * DV:(t + 1) * DV])
                wait_root()
                cols = slice(hd * DV, (hd + 1) * DV)
                for bb in plan["cd4" if hd < 2 else "cd5"]:
                    wait_stored(dve, "cd4" if hd < 2 else "cd5", bb)
                for t in range(TB):
                    ins = V.scalar_tensor_tensor(out=tok[:, 1, t, cols], in0=bank[b][:, t * DV:(t + 1) * DV],
                                                 scalar=rstd[:, t:t + 1], in1=tok[:, 1, t, cols],
                                                 op0=ALU.mult, op1=ALU.mult)
                    ins.then_inc(stored[b], 1) if t else step(ins)

            gla_head(0)
            p_gla(0)
            gla_head(1)
            p_gla(1)
            cw = ROWS_CD["conv_w"]
            y_gla(0)
            y_gla(1)
            taps("cd6", 8, cols_cd, cw, 16, 0, 8)
            gla_head(2)
            p_gla(2)
            gla_head(3)
            p_gla(3)
            y_gla(2)
            y_gla(3)
            taps("cd7", 12, cols_cd, cw, 16, 4, 12)
            taps("cd8", 16, cols_cd, cw, 16, 8, 16)
            taps("cd9", 20, cols_cd, cw, 16, 12, 20)
            for n in range(4):
                for q, b in enumerate(plan[f"xs_turn{n}"]):
                    wait_ready(dve, f"xs_turn{n}", b)
                    t, c0 = n // 2, 4 * (n % 2) + 2 * q
                    heads = lambda x: x.rearrange("p (n d) -> p n d", d=SSD_HD)
                    nh = 2 * P // SSD_HD
                    h0 = c0 * P // SSD_HD
                    wide = lambda x: x.rearrange("p (n o) -> p n o", o=1).to_broadcast([P, nh, SSD_HD])
                    link(V.tensor_tensor(heads(tok[:, 2, t, c0 * P:(c0 + 2) * P]), heads(bank[b][:, 0:2 * P]),
                                         wide(ssd_d[:, h0:h0 + nh]), ALU.mult))
                    V.tensor_tensor(heads(xdt[:, t, c0 * P:(c0 + 2) * P]), heads(bank[b][:, 0:2 * P]),
                                    wide(gate_col[:, 1, t, h0:h0 + nh]), ALU.mult).then_inc(stored[b], 1)
            for g in range(GROUPS):
                decay_args(f"cum{g}", lambda r, j: route[:, 5, j, 4 * g + r:4 * g + r + 1],
                           lambda r: dec[:, r, :], 0)
                sbk, yb = first_of(f"s_ssd{g}"), first_of(f"y_ssd{g}")
                for r in range(4):
                    hd = 4 * g + r
                    if r >= 2:
                        dve.wait_ge(kused, 28 + 3 * g + r - 1)
                    elif g:
                        dve.wait_ge(kused, 28 + 3 * g)
                        wait_ready(dve, f"y_ssd{g - 1}", first_of(f"y_ssd{g - 1}"))
                    ins = decayed(f"s_ssd{g}", sbk, hd, 1.0, dec[:, r, :], 12 + hd + 1)
                    ins.then_inc(prob_ready if r < 3 else stored[sbk], 1)
                wait_ready(dve, f"y_ssd{g}", yb)
                cols = slice(g * DV, (g + 1) * DV)
                if g == 0:
                    for u in (10, 11):
                        for bb in plan[f"cd{u}"]:
                            wait_stored(dve, f"cd{u}", bb)
                for t in range(TB):
                    ins = V.tensor_tensor(tok[:, 2, t, cols], bank[yb][:, t * DV:(t + 1) * DV],
                                          tok[:, 2, t, cols], ALU.add)
                    ins.then_inc(stored[yb], 1) if t else step(ins)
                wait_stored(dve, f"y_ssd{g}", yb)
                for t in range(TB):
                    link(V.tensor_tensor(tok[:, 3, t, cols], tok[:, 3, t, cols], tok[:, 2, t, cols], ALU.mult))
                square_mean(lambda t: tok[:, 3, t, cols])
                wait_root()
                for t in range(TB):
                    ins = V.tensor_scalar(tok[:, 3, t, cols], tok[:, 3, t, cols], rstd[:, t:t + 1], None, ALU.mult)
                    link(ins) if t == 0 else ins.then_inc(y_done, 1)
                dve.wait_ge(y_done, 8 + g + 1)
            y_turns(1, cols_cd)
            layernorm(add_mix(1), 2 * TB)
            if stop_after == "mix1":
                return
            moe(1)


_INS = ["x", "positions", "w_in_ab", "ret_norm_g", "ml_conv_w", "ml_conv_b", "ml_b_i", "ml_b_f", "ml_norm_g",
        "w_out_ab", "w_in_cd", "gla_w_alpha", "gla_b_alpha", "gla_norm_g", "ssd_conv_w", "ssd_conv_b",
        "ssd_dt_bias", "ssd_a_log", "ssd_d", "ssd_norm_g", "w_out_cd", "w_router", "b_router", "moe_w_gate",
        "moe_w_up", "moe_w_down", "ln_mix_g", "ln_mix_b", "ln_ffn_g", "ln_ffn_b"]
STOP = None


def kernel(**inputs):
    import concourse.bacc as _bacc
    from concourse.bass_utils import run_bass_kernel_spmd as _run

    nc = _bacc.Bacc("TRN2", target_bir_lowering=False, num_devices=1)
    arrays, aps = {}, {}
    for name in _INS + ["consts"]:
        v = np.ascontiguousarray(shape_constants() if name == "consts" else inputs[name])
        arrays[f"in_{name}"] = v
        aps[name] = nc.dram_tensor(f"in_{name}", v.shape, mybir.dt.from_np(v.dtype), kind="ExternalInput").ap()
    out = nc.dram_tensor("out_0", (1, SEQ, D), F32, kind="ExternalOutput").ap()
    build(nc, aps, out, STOP)
    r = _run(nc, [arrays], core_ids=[0])
    return r.results[0]["out_0"]
```

```python
from contextlib import ExitStack

import numpy as np

import concourse.bass as bass
from concourse import mybir

F32 = mybir.dt.float32
I32 = mybir.dt.int32
ALU = mybir.AluOpType
ACT = mybir.ActivationFunctionType
AX = mybir.AxisListType

P = 128
SEQ = 256
TB = SEQ // P
D = 1024
KC = D // P
UNIT = 512
HEADS = 4
DK = 128
DV = 256
FF = 512
EXPERTS = 16
GROUPS = 4
PER_GROUP = EXPERTS // GROUPS
SSD_HEADS = 16
SSD_HD = 64
GLA_RANK = 16
MIX = 2048
DEPTH = 2
CAUSAL = SEQ + P
LN_EPS = 1e-5
NORM_EPS = 1e-6
ALPHA = 4.0 ** 0.25
QK_SCALE = float(DK) ** -0.5
GLA_TAU = 16.0
GLA_BLOCK = 32
GLA_MID = 15
GLA_CAP = float(np.exp(35.0))
RING = 6
BLOCK = 64
PAIRS = EXPERTS // 2
ROWS = 2 * BLOCK
PASSES = SEQ // BLOCK
MOE_USES = (3, 3, 5, 5)
QUADS = PAIRS // 2
TWO_PI = 2.0 * np.pi
ROUND = 12582912.0
PI_A = 6.28125
PI_B = float(np.float32(np.round((TWO_PI - PI_A) * 2 ** 22) / 2 ** 22))
PI_C = float(TWO_PI - PI_A - PI_B)
PI_SAFE = 3.1415925
LOG_GAMMA = [float(np.log(1.0 - 2.0 ** (-5.0 - h))) for h in range(HEADS)]

C_ID, C_CAP, C_MASK, C_DIST = 0, 128, 128 + CAUSAL, 128 + 2 * CAUSAL
C_FREQ = 128 + 3 * CAUSAL
C_PRI = C_FREQ + 1
C_IOTA = C_PRI + EXPERTS
C_ALL = C_IOTA + BLOCK


def shape_constants():
    c = np.zeros((P, C_ALL), np.float32)
    c[:, C_ID:C_ID + P] = np.eye(P)
    s = np.arange(P)[:, None]
    dist = np.concatenate([np.arange(SEQ)[None, :] - s, np.arange(P)[None, :] - s], axis=1)
    c[:, C_CAP:C_CAP + CAUSAL] = np.where(dist >= 0, 0.0, -1e30)
    c[:, C_MASK:C_MASK + CAUSAL] = dist >= 0
    c[:, C_DIST:C_DIST + CAUSAL] = np.where(dist >= 0, dist, 1e5)
    half = np.arange(P) % (DK // 2)
    c[:, C_FREQ] = np.float32(10000.0) ** (-(2 * half).astype(np.float32) / np.float32(DK))
    c[:, C_PRI:C_PRI + EXPERTS] = EXPERTS - np.arange(EXPERTS)
    c[:, C_IOTA:C_IOTA + BLOCK] = 1 + np.arange(BLOCK)
    return c


AB_UNITS = [("w_in_ab", c) for c in
            [0, 512,
             1024, 1536, 2048, 2560,
             3072, 3584,
             4096, 4608, 5120, 5632]]
AB_TAIL = 6144
CD_UNITS = [("w_in_cd", c) for c in
            [0, 512,
             1024, 1536, 2048, 2560,
             4112, 4624, 5136, 5648,
             3088, 3600]]
CD_TAIL_A, CD_TAIL_DT = 3072, 6160
OUT_UNITS = 4
LAYER_UNITS = len(AB_UNITS) + OUT_UNITS
MOE_UNITS = 3 * EXPERTS
ROWS_AB = dict(norm=0, conv_w=16, conv_b=48, n=56)
ROWS_CD = dict(norm=0, conv_w=16, conv_b=80, b_alpha=96, n=100)


def build(nc, a, out):
    with ExitStack() as ctx:
        def sb(name, shape, dt=F32):
            return ctx.enter_context(nc.sbuf_tensor(name, shape, dt))

        def sem(name):
            return ctx.enter_context(nc.semaphore(name))

        ctx.enter_context(nc.allow_non_contiguous_dma(reason="a few small parameter loads"))
        bank = [ctx.enter_context(nc.psum_tensor(f"bank{i}", [P, 512], F32)) for i in range(8)]

        ring = sb("ring", [P, RING, KC * UNIT])
        consts = sb("consts", [P, C_ALL])
        h = sb("h", [P, TB, D])
        hT = sb("hT", [P, KC, SEQ])
        feat = sb("feat", [P, 24, SEQ])
        tok = sb("tok", [P, 4, TB, D])
        yT = sb("yT", [P, MIX // P, SEQ])
        rows_ab = sb("rows_ab", [ROWS_AB["n"], P])
        rows_cd = sb("rows_cd", [ROWS_CD["n"], P])
        cols_ab = sb("cols_ab", [P, ROWS_AB["n"]])
        cols_cd = sb("cols_cd", [P, ROWS_CD["n"]])
        tail_ab = sb("tail_ab", [P, KC, 2 * HEADS])
        tail_a = sb("tail_a", [P, KC, GLA_RANK])
        tail_dt = sb("tail_dt", [P, KC, SSD_HEADS])
        w_alpha = sb("w_alpha", [GLA_RANK, HEADS * DK])
        w_router = sb("w_router", [P, KC, EXPERTS])
        b_router = sb("b_router", [P, TB, EXPERTS])
        ml_bias = sb("ml_bias", [HEADS, 2])
        ssd_par = sb("ssd_par", [SSD_HEADS, 2])
        ssd_d = sb("ssd_d", [P, SSD_HEADS])
        prob = sb("prob", [P, 2, CAUSAL])
        gate_row = sb("gate_row", [16, 5, SEQ])
        ones_row = sb("ones_row", [16, SEQ])
        ones_col = sb("ones_col", [P, 1])
        gate_col = sb("gate_col", [P, 2, TB, 16])
        stat = sb("stat", [P, 8, 6])
        mv = sb("mv", [P, TB, 2])
        rstd = sb("rstd", [P, TB])
        rec = sb("rec", [P, TB])
        eps = sb("eps", [P, 2])
        route = sb("route", [P, 8, TB, EXPERTS])
        rsmall = sb("rsmall", [P, 6, TB, GROUPS])
        rank = sb("rank", [P, TB, EXPERTS])
        load_f = sb("load_f", [P, 1])
        load_i = sb("load_i", [P, 1], I32)
        zero_row = sb("zero_row", [1, P])

        ident = consts[:, C_ID:C_ID + P]
        cap = consts[:, C_CAP:C_CAP + CAUSAL]
        cmask = consts[:, C_MASK:C_MASK + CAUSAL]
        dist = consts[:, C_DIST:C_DIST + CAUSAL]
        pri = consts[:, C_PRI:C_PRI + EXPERTS]
        trig = yT[:, 0:4, :].rearrange("p a t -> p (a t)").rearrange("p (a n) -> p a n", n=512)
        pos_i = yT[:, 4, :].bitcast(I32)
        pos_f = yT[:, 5, :]
        angle = yT[:, 6, :]
        turns = yT[:, 7:9, :]
        rot = yT[:, 10:14, :].rearrange("p a t -> p (a t)").rearrange("p (a n) -> p a n", n=512)
        bcum = yT[:, 8:12, :]
        gtmp = yT[:, 12:16, :]
        xdt = yT[:, 8:16, :].rearrange("p a t -> p (a t)").rearrange("p (b n) -> p b n", b=TB)
        dec = yT[:, 0:6, :].rearrange("p a t -> p (a t)").rearrange("p (r n) -> p r n", n=CAUSAL)
        ssd_dec = feat[:, 0:6, :].rearrange("p a t -> p (a t)").rearrange("p (r n) -> p r n", n=CAUSAL)
        mlexp = feat[:, 16:22, :].rearrange("p a t -> p (a t)").rearrange("p (r n) -> p r n", n=CAUSAL)
        flat = lambda x: x.rearrange("p a t -> p (a t)")
        xg = feat[:, 0:8, :]
        sil = flat(feat[:, 8:10, :])
        hid = flat(feat[:, 10:12, :])
        hid_t = flat(feat[:, 12:14, :]).rearrange("p (k n) -> p k n", n=P)
        ye = flat(feat[:, 14:18, :])
        selw = feat[:, 18, :].rearrange("p (t n) -> p t n", n=P)
        selw_t = feat[:, 19:21, :]
        sel = tok[:, 1, :, :].rearrange("p t n -> p (t n)")[:, 0:TB * EXPERTS * BLOCK] \
            .rearrange("p (t e n) -> p t e n", t=TB, e=EXPERTS)
        as_unit = lambda x: flat(x).rearrange("p (k n) -> p k n", n=FF)
        early = ((as_unit(yT[:, 0:8, :]), as_unit(yT[:, 8:16, :])),
                 (as_unit(tok[:, 0, :, :]), as_unit(tok[:, 3, :, :])),
                 (as_unit(tok[:, 2, :, :]), as_unit(hT)))
        EARLY = len(early)
        lnp = tok[:, 2, :, :]

        ready = [sem(f"bank{i}_ready") for i in range(8)]
        stored = [sem(f"bank{i}_stored") for i in range(8)]
        ring_full = [sem(f"ring_full{i}") for i in range(RING)]
        early_in = sem("early_in")
        out_used = sem("out_used")
        par_in = sem("par_in")
        par_late = sem("par_late")
        x_in = sem("x_in")
        ln_in = sem("ln_in")
        ln_ffn_in = sem("ln_ffn_in")
        dve_step = sem("dve_step")
        act_step = sem("act_step")
        out_done = sem("out_done")
        h_ready = sem("h_ready")
        trig_arg = sem("trig_arg")
        trig_done = sem("trig_done")
        dec_arg = sem("dec_arg")
        dec_done = sem("dec_done")
        prob_ready = sem("prob_ready")
        rot_ready = sem("rot_ready")
        conv_first = sem("conv_first")
        conv_sum = sem("conv_sum")
        gate_a = sem("gate_a")
        gate_b = sem("gate_b")
        gate_ok = sem("gate_ok")
        var_ready = sem("var_ready")
        rstd_ready = sem("rstd_ready")
        y_done = sem("y_done")
        kscale = sem("kscale")
        kexp = sem("kexp")
        kused = sem("kused")
        r_exp = sem("r_exp")
        rank_in = sem("rank_in")
        load_ready = sem("load_ready")

        class Pass:

            def __init__(self, tag, main=None):
                self.main = main is not None
                self.ready = ready if self.main else [sem(f"more{tag}_bank{i}_ready") for i in range(4)]
                self.stored = stored if self.main else [sem(f"more{tag}_bank{i}_stored") for i in range(4)]
                self.full = ring_full if self.main else [sem(f"more{tag}_full{i}") for i in range(RING)]
                self.selw = sem(f"selw{tag}_ready")
                self.sel = sem(f"sel{tag}_ready")
                self.base = main or {b: 0 for b in range(4)}
                self.next = None if self.main else sem(f"more{tag}_next")
                self.slots = None if self.main else sem(f"more{tag}_slots")

            def filled(self, eng, i, b, k):
                eng.wait_ge(self.ready[b], i * MOE_USES[b] + (self.base[b] + k + 1))

            def read(self, eng, i, b, k):
                eng.wait_ge(self.stored[b], i * MOE_USES[b] + (self.base[b] + k + 1))

            def claim(self, eng, i, b, k):
                if self.main or k:
                    eng.wait_ge(self.stored[b], i * MOE_USES[b] + (self.base[b] + k))

        uses = [0] * 8
        plan = {}

        def job(name, *banks):
            plan[name] = {b: uses[b] for b in banks}
            for b in banks:
                uses[b] += 1

        flip = [0]
        passes = {}

        def pair_job(name):
            job(name, *((0, 1), (2, 3))[flip[0] % 2])
            flip[0] += 1

        def single_job(name):
            job(name, (0, 2)[flip[0] % 2])
            flip[0] += 1

        def turn_jobs(tag):
            pair_job(tag + "0")
            pair_job(tag + "1")

        def moe_jobs(layer):
            job(f"router{layer}", 4)
            job(f"rank{layer}", 4)
            base = dict(enumerate(uses[0:4]))
            for b in range(4):
                uses[b] += QUADS * MOE_USES[b]
            job(f"ffn{layer}", 4, 5, 6, 7)
            passes[layer] = Pass(layer, base), Pass(f"{layer}b")

        turn_jobs("x_turn")
        pair_job("params")
        for n in range(2):
            pair_job(f"ab{n}")
        single_job("gates")
        for n in (2, 3):
            pair_job(f"ab{n}")
        single_job("gate_cols")
        pair_job("gate_rows")
        for n in (4, 5):
            pair_job(f"ab{n}")
        for hd in range(2):
            job(f"s_ret{hd}", 4 + hd % 2)
        pair_job("ab6")
        for hd in range(2):
            job(f"y_ret{hd}", 6 + hd % 2)
        for hd in range(2, 4):
            job(f"s_ret{hd}", 4 + hd % 2)
        pair_job("ab7")
        for hd in range(2, 4):
            job(f"y_ret{hd}", 6 + hd % 2)
        pair_job("ab8")
        pair_job("ab9")
        pair_job("yturn0_0")
        pair_job("yturn0_1")
        for hd in range(2):
            job(f"s_ml{hd}", 4 + hd % 2)
        pair_job("ab10")
        for hd in range(2):
            job(f"y_ml{hd}", 6 + hd % 2)
        for hd in range(2, 4):
            job(f"s_ml{hd}", 4 + hd % 2)
        pair_job("ab11")
        for hd in range(2, 4):
            job(f"y_ml{hd}", 6 + hd % 2)
        job("mix0", 0, 1, 2, 3)
        job("yturn0_2", 4, 5)
        job("yturn0_3", 6, 7)
        turn_jobs("mix_turn0_")
        moe_jobs(0)
        turn_jobs("ffn_turn0_")

        for n in range(2):
            pair_job(f"cd{n}")
        pair_job("alpha_in")
        pair_job("alpha")
        single_job("dt_cols")
        for n in range(2, 6):
            pair_job(f"cd{n}")
        for hd in range(2):
            job(f"s_gla{hd}", 4 + hd % 2)
        pair_job("cd6")
        for hd in range(2):
            job(f"y_gla{hd}", 6 + hd % 2)
        pair_job("cd7")
        for hd in range(2, 4):
            job(f"s_gla{hd}", 4 + hd % 2)
        pair_job("cd8")
        for hd in range(2, 4):
            job(f"y_gla{hd}", 6 + hd % 2)
        for n in range(9, 12):
            pair_job(f"cd{n}")
        pair_job("yturn1_0")
        pair_job("yturn1_1")
        for n in range(4):
            pair_job(f"xs_turn{n}")
        job("mix1", 0, 1, 2, 3)
        for g in range(GROUPS):
            job(f"cum{g}", 4, 5)
            job(f"s_ssd{g}", 6)
            job(f"y_ssd{g}", 7)
        job("yturn1_2", 4, 5)
        job("yturn1_3", 6, 7)
        turn_jobs("mix_turn1_")
        moe_jobs(1)

        def first_of(name):
            return min(plan[name])

        def wait_ready(eng, name, b):
            eng.wait_ge(ready[b], plan[name][b] + 1)

        def wait_stored(eng, name, b):
            eng.wait_ge(stored[b], plan[name][b] + 1)

        def unit_no(layer, n):
            return layer * (LAYER_UNITS + MOE_UNITS) + n

        tok_sets = {"ab2": (0, 0), "ab3": (0, 1), "ab4": (1, 0), "ab5": (1, 1), "ab8": (2, 0), "ab9": (2, 1),
                    "ab10": (3, 0), "ab11": (3, 1), "cd2": (0, 0), "cd3": (0, 1), "cd4": (1, 0), "cd5": (1, 1),
                    "cd10": (3, 0), "cd11": (3, 1)}

        def freed(n):
            layer, u = divmod(n, LAYER_UNITS + MOE_UNITS)
            if u < 12:
                name = ("ab", "cd")[layer] + str(u)
                b = max(plan[name])
                return ready[b], plan[name][b] + 1
            if u < LAYER_UNITS - 1:
                return out_used, layer * (OUT_UNITS - 1) + u - 11
            if u == LAYER_UNITS - 1:
                return ready[3], plan[f"mix{layer}"][3] + 1
            i, j = divmod(u - LAYER_UNITS, 6)
            if j < EARLY:
                i = min(i, PAIRS - 2)
            b = 2 if j < 2 else 3
            use = (1 if j < 4 else 2) + 2 * (i % 2)
            return ready[b], passes[layer][0].base[b] + MOE_USES[b] * (i // 2) + use + 1

        def landed(n):
            skipped = n >= unit_no(1, 0) and n % RING in [unit_no(0, LAYER_UNITS + j) % RING for j in range(EARLY)]
            return 16 * (n // RING + 1 - skipped)

        par_list = [
            (consts[:, :], a["consts"]),
            (pos_i, a["positions"].to_broadcast([P, SEQ])),
            (rows_ab[0:8, :], a["ret_norm_g"].rearrange("o (k p) -> (o k) p", p=P)),
            (rows_ab[8:16, :], a["ml_norm_g"].rearrange("o (k p) -> (o k) p", p=P)),
            (rows_ab[16:48, :], a["ml_conv_w"].rearrange("o t (k p) -> (o t k) p", p=P)),
            (rows_ab[48:56, :], a["ml_conv_b"].rearrange("o (k p) -> (o k) p", p=P)),
            (rows_cd[0:8, :], a["gla_norm_g"].rearrange("o (k p) -> (o k) p", p=P)),
            (rows_cd[8:16, :], a["ssd_norm_g"].rearrange("o (k p) -> (o k) p", p=P)),
            (rows_cd[16:80, :], a["ssd_conv_w"].rearrange("o t (k p) -> (o t k) p", p=P)),
            (rows_cd[80:96, :], a["ssd_conv_b"].rearrange("o (k p) -> (o k) p", p=P)),
            (rows_cd[96:100, :], a["gla_b_alpha"].rearrange("o (k p) -> (o k) p", p=P)),
            (tail_ab[:, :, :], a["w_in_ab"][0, :, AB_TAIL:AB_TAIL + 2 * HEADS].rearrange("(k p) n -> p k n", p=P)),
            (tail_a[:, :, :], a["w_in_cd"][0, :, CD_TAIL_A:CD_TAIL_A + GLA_RANK].rearrange("(k p) n -> p k n", p=P)),
            (tail_dt[:, :, :],
             a["w_in_cd"][0, :, CD_TAIL_DT:CD_TAIL_DT + SSD_HEADS].rearrange("(k p) n -> p k n", p=P)),
            (w_alpha[:, :], a["gla_w_alpha"][0]),
            (w_router[:, :, :], a["w_router"].rearrange("(k p) n -> p k n", p=P)),
            (b_router[:, 0, :], a["b_router"].rearrange("(o n) -> o n", o=1).to_broadcast([P, EXPERTS])),
            (b_router[:, 1, :], a["b_router"].rearrange("(o n) -> o n", o=1).to_broadcast([P, EXPERTS])),
            (ml_bias[:, 0:1], a["ml_b_i"].rearrange("o n -> n o")),
            (ml_bias[:, 1:2], a["ml_b_f"].rearrange("o n -> n o")),
            (ssd_par[:, 0:1], a["ssd_dt_bias"].rearrange("o n -> n o")),
            (ssd_par[:, 1:2], a["ssd_a_log"].rearrange("o n -> n o")),
            (ssd_d[:, :], a["ssd_d"].to_broadcast([P, SSD_HEADS])),
        ]
        PAR_FIRST = 11

        block = ctx.enter_context(nc.Block())

        @block.sync
        def _(sp):
            def load(par, count):
                for dst, src in par:
                    sp.dma_start(dst, src).then_inc(count, 16)

            load(par_list[0:1], par_in)
            for b in range(TB):
                sp.dma_start(h[:, b, :], a["x"][0, b * P:(b + 1) * P, :]).then_inc(x_in, 16)
            load(par_list[1:PAR_FIRST], par_in)

            def stream(n, dst, src):
                if n >= RING:
                    sp.wait_ge(*freed(n - RING))
                sp.dma_start(dst, src).then_inc(ring_full[n % RING], 16)

            def slot(n, k):
                return ring[:, n % RING, :].rearrange("p (k n) -> p k n", k=k)

            for layer, (units, w_out) in enumerate(((AB_UNITS, "w_out_ab"), (CD_UNITS, "w_out_cd"))):
                for u, (name, c0) in enumerate(units):
                    n = unit_no(layer, u)
                    stream(n, slot(n, KC), a[name][0, :, c0:c0 + UNIT].rearrange("(k p) n -> p k n", p=P))
                    if n == 0:
                        load(par_list[PAR_FIRST:], par_late)
                wo = a[w_out][0].rearrange("(k p) n -> p k n", p=P)
                for u in range(OUT_UNITS):
                    n = unit_no(layer, len(units) + u)
                    stream(n, slot(n, 4), wo[:, 4 * u:4 * u + 4, :])
                n0 = unit_no(layer, LAYER_UNITS)
                gate = a["moe_w_gate"].rearrange("l e (k p) n -> l e p k n", p=P)
                up = a["moe_w_up"].rearrange("l e (k p) n -> l e p k n", p=P)
                down = a["moe_w_down"].rearrange("l e (k p) n -> l e p k n", p=P)
                pair = ((gate, 0, KC), (gate, 1, KC), (up, 0, KC), (up, 1, KC), (down, 0, FF // P),
                        (down, 1, FF // P))
                for j, (src, e, k) in enumerate(pair):
                    stream(n0 + j, slot(n0 + j, k), src[layer, e])
                for j, (src, e, k) in enumerate(pair[0:EARLY]):
                    unit = src[layer, 2 * PAIRS - 2 + e]
                    for half in range(2):
                        if j == 2 and half == 0:
                            sp.wait_ge(h_ready, TB * (2 * layer + 1))
                        if j == 2 and half == 1:
                            wait_ready(sp, f"router{layer}", 4)
                        sp.dma_start(early[j][half], unit[:, half * (KC // 2):(half + 1) * (KC // 2), :]) \
                            .then_inc(early_in, 16)
                for j, (src, e, k) in enumerate(pair):
                    stream(n0 + 6 + j, slot(n0 + j, k), src[layer, 2 + e])
                with sp.Fori(1, QUADS - 1) as i:
                    for half in range(2):
                        for j, (src, e, k) in enumerate(pair):
                            n = n0 + 12 + 6 * half + j
                            done, count = freed(n - RING)
                            sp.wait_ge(done, i * MOE_USES[2] + (count - MOE_USES[2]))
                            sp.dma_start(slot(n, k), src[layer, i * 4 + (2 * half + e)]) \
                                .then_inc(ring_full[n % RING], 16)
                for i in (PAIRS - 2, PAIRS - 1):
                    for j, (src, e, k) in enumerate(pair):
                        n = n0 + 6 * i + j
                        if i < PAIRS - 1 or j >= EARLY:
                            stream(n, slot(n, k), src[layer, 2 * i + e])
                sp.wait_ge(ready[3], passes[layer][0].base[3] + MOE_USES[3] * (QUADS - 1) + 4)
                for k, name in enumerate(("ln_ffn_g", "ln_ffn_b")):
                    sp.dma_start(lnp[:, k, :], a[name][layer:layer + 1, :].to_broadcast([P, D])) \
                        .then_inc(ln_ffn_in, 16)
                sp.wait_ge(load_ready, layer + 1)
                load = sp.value_load(load_i[0:1, 0:1], min_val=0, max_val=SEQ)
                with sp.If(load > BLOCK):
                    for j in range(6):
                        sp.wait_ge(*freed(n0 + 6 * (PAIRS - 1) + j))
                    more = passes[layer][1]
                    with sp.Fori(0, PASSES - 1) as p:
                        with sp.Fori(0, QUADS) as i:
                            for half in range(2):
                                sp.wait_ge(more.slots, p * PAIRS + i * 2 + (half + 1))
                                for j, (src, e, k) in enumerate(pair):
                                    n = n0 + j
                                    sp.dma_start(slot(n, k), src[layer, i * 4 + (2 * half + e)]) \
                                        .then_inc(more.full[n % RING], 16)
                    sp.wait_ge(more.slots, (PASSES - 1) * PAIRS + 1)
            last = 2 * DEPTH
            for b in range(TB):
                sp.wait_ge(h_ready, TB * (last - 1) + b + 1)
                sp.dma_start(out[0, b * P:(b + 1) * P, :], h[:, b, :]).then_inc(out_done, 16)
            sp.wait_ge(out_done, 16 * TB)

        @block.gpsimd
        def _(pool):
            for layer in range(DEPTH):
                pool.wait_ge(y_done, (8, 12)[layer])
                for k, name in enumerate(("ln_mix_g", "ln_mix_b")):
                    pool.dma_start(lnp[:, k, :], a[name][layer:layer + 1, :].to_broadcast([P, D])).then_inc(ln_in, 16)

        @block.tensor
        def _(pe):
            def claim(name, b):
                if plan[name][b]:
                    pe.wait_ge(stored[b], plan[name][b])

            def mm(o, l, r, start=True, stop=True):
                return nc.tensor.matmul(o, l, r, start=start, stop=stop)

            def turn_h(tag, n_ready=None):
                for t in range(TB):
                    if n_ready is not None:
                        pe.wait_ge(h_ready, n_ready + t + 1)
                    for j in range(2):
                        for q, b in enumerate(plan[f"{tag}{j}"]):
                            if t == 0:
                                claim(f"{tag}{j}", b)
                            k0 = 4 * j + 2 * q
                            for k in range(2):
                                last = nc.tensor.transpose(bank[b][:, k * SEQ + t * P:k * SEQ + (t + 1) * P],
                                                           h[:, t, (k0 + k) * P:(k0 + k + 1) * P], ident)
                            if t == TB - 1:
                                last.then_inc(ready[b], 1)

            def wait_hT(tag):
                for j in range(2):
                    for b in plan[f"{tag}{j}"]:
                        wait_stored(pe, f"{tag}{j}", b)

            def unit_in(n):
                pe.wait_ge(ring_full[n % RING], landed(n))

            def feature_unit(name, n, columns):
                unit_in(n)
                w = ring[:, n % RING, :].rearrange("p (k n) -> p k n", k=KC)
                for q, b in enumerate(plan[name]):
                    claim(name, b)
                    for m in (2 * q, 2 * q + 1):
                        for k in range(KC):
                            last = mm(bank[b][:, (m % 2) * SEQ:(m % 2 + 1) * SEQ], columns(w, k, m), hT[:, k, :],
                                      k == 0, k == KC - 1)
                    last.then_inc(ready[b], 1)

            def token_unit(name, n):
                unit_in(n)
                w = ring[:, n % RING, :].rearrange("p (k n) -> p k n", k=KC)
                for t, b in enumerate(plan[name]):
                    claim(name, b)
                    for k in range(KC):
                        last = mm(bank[b][:, :], hT[:, k, t * P:(t + 1) * P], w[:, k, :], k == 0, k == KC - 1)
                    last.then_inc(ready[b], 1)

            plain = lambda w, k, m: w[:, k, m * P:(m + 1) * P]
            pairs = lambda w, k, m: w[:, k, (m // 2) * SEQ + m % 2:(m // 2 + 1) * SEQ:2]

            def weights_out(layer, u, blocks=range(TB)):
                n = unit_no(layer, 12 + u)
                unit_in(n)
                w = ring[:, n % RING, :].rearrange("p (k n) -> p k n", k=4)
                for t in blocks:
                    for k in range(4):
                        for half in range(2):
                            b = 2 * t + half
                            if u == 0 and k == 0:
                                claim(f"mix{layer}", b)
                            last = mm(bank[b][:, :], yT[:, 4 * u + k, t * P:(t + 1) * P],
                                      w[:, k, half * 512:(half + 1) * 512],
                                      u == 0 and k == 0, u == OUT_UNITS - 1 and k == 3)
                            if u == OUT_UNITS - 1 and k == 3:
                                last.then_inc(ready[b], 1)
                if u < OUT_UNITS - 1 and t == TB - 1:
                    last.then_inc(out_used, 1)

            def y_turn(layer, n):
                name = f"yturn{layer}_{n}"
                if layer and n < 2:
                    wait_stored(pe, "y_gla3", first_of("y_gla3"))
                else:
                    pe.wait_ge(y_done, 8 * layer + (4, 4, 2 + 4 * (1 - layer), 4 + 4 * (1 - layer))[n])
                src = tok[:, 1 if n < 2 else 3, :, :]
                for q, b in enumerate(plan[name]):
                    claim(name, b)
                    for k in range(2):
                        c = (4 * n + 2 * q + k) % 8
                        for t in range(TB):
                            last = nc.tensor.transpose(bank[b][:, k * SEQ + t * P:k * SEQ + (t + 1) * P],
                                                       src[:, t, c * P:(c + 1) * P], ident)
                    last.then_inc(ready[b], 1)

            def values(b, v, slots, start_cols=0, width=DV):
                for t in range(TB):
                    for j in range(t + 1):
                        lhs = slots[:, t * P:(t + 1) * P] if j == 0 else slots[:, SEQ:SEQ + P]
                        last = mm(bank[b][:, t * DV + start_cols:t * DV + start_cols + width], lhs, v(j),
                                  j == 0, j == t)
                return last

            def score_group(b, kk, qq, parts, start=True, stop=True):
                for j in range(2):
                    last = mm(bank[b][:, j * SEQ:j * SEQ + SEQ - j * P], kk[parts, j * P:(j + 1) * P],
                              qq[parts, j * P:SEQ], start, stop)
                return last

            full = slice(0, P)

            pe.wait_ge(x_in, 16 * TB)
            pe.wait_ge(par_in, 16 * PAR_FIRST)
            pe.wait_ge(dve_step, 3)
            turn_h("x_turn")
            for (src, n_rows), b in zip(((rows_ab, ROWS_AB["n"]), (rows_cd, ROWS_CD["n"])), plan["params"]):
                claim("params", b)
                nc.tensor.transpose(bank[b][:, 0:n_rows], src[:, :], consts[0:n_rows, C_ID:C_ID + n_rows]) \
                    .then_inc(ready[b], 1)
            wait_hT("x_turn")
            feature_unit("ab0", unit_no(0, 0), pairs)
            feature_unit("ab1", unit_no(0, 1), pairs)

            pe.wait_ge(par_late, 16 * (len(par_list) - PAR_FIRST))
            bs = list(plan["gates"])
            claim("gates", bs[0])
            for q in range(2):
                for k in range(KC):
                    last = mm(bank[bs[0]][0:HEADS, q * SEQ:(q + 1) * SEQ],
                              tail_ab[:, k, q * HEADS:(q + 1) * HEADS], hT[:, k, :], k == 0, k == KC - 1)
            last.then_inc(ready[bs[0]], 1)

            def gate_turns():
                b0 = first_of("gate_cols")
                claim("gate_cols", b0)
                pe.wait_ge(gate_ok, 1)
                for q, row in enumerate((2, 4)):
                    for t in range(TB):
                        last = nc.tensor.transpose(bank[b0][:, (q * TB + t) * 16:(q * TB + t) * 16 + HEADS],
                                                   gate_row[0:HEADS, row, t * P:(t + 1) * P],
                                                   consts[0:HEADS, C_ID:C_ID + HEADS])
                last.then_inc(ready[b0], 1)
                for q, b in enumerate(plan["gate_rows"]):
                    claim("gate_rows", b)
                    for hd in (2 * q, 2 * q + 1):
                        last = mm(bank[b][:, (hd % 2) * SEQ:(hd % 2 + 1) * SEQ],
                                  consts[0:HEADS, C_ID + hd:C_ID + hd + 1].to_broadcast([HEADS, P]),
                                  gate_row[0:HEADS, 3, :])
                    last.then_inc(ready[b], 1)

            for u in (2, 3):
                token_unit(f"ab{u}", unit_no(0, u))
            gate_turns()
            for u in (4, 5):
                token_unit(f"ab{u}", unit_no(0, u))

            def s_ret(hd):
                b = first_of(f"s_ret{hd}")
                claim(f"s_ret{hd}", b)
                pe.wait_ge(rot_ready, 4)
                hp, part = hd // 2, slice(64 * (hd % 2), 64 * (hd % 2) + 64)
                for j in range(2):
                    for c in range(2):
                        last = mm(bank[b][:, j * SEQ:j * SEQ + SEQ - j * P],
                                  feat[part, 4 + 2 * hp + c, j * P:(j + 1) * P],
                                  feat[part, 2 * hp + c, j * P:SEQ], c == 0, c == 1)
                last.then_inc(ready[b], 1)

            def y_ret(hd):
                b = first_of(f"y_ret{hd}")
                claim(f"y_ret{hd}", b)
                wait_stored(pe, f"s_ret{hd}", first_of(f"s_ret{hd}"))
                if hd == 0:
                    for u in (2, 3):
                        for bb in plan[f"ab{u}"]:
                            wait_stored(pe, f"ab{u}", bb)
                values(b, lambda j: tok[:, 0, j, hd * DV:(hd + 1) * DV],
                       slots=prob[:, hd % 2, :]).then_inc(ready[b], 1)

            def s_ml(hd):
                b = first_of(f"s_ml{hd}")
                claim(f"s_ml{hd}", b)
                if hd == 0:
                    for u in (6, 7):
                        for bb in plan[f"ab{u}"]:
                            wait_stored(pe, f"ab{u}", bb)
                score_group(b, feat[:, 12 + hd, :], feat[:, 8 + hd, :], full).then_inc(ready[b], 1)

            def y_ml(hd):
                b, bd = first_of(f"y_ml{hd}"), first_of(f"s_ml{hd}")
                claim(f"y_ml{hd}", b)
                pe.wait_ge(prob_ready, hd + 1)
                if hd == 0:
                    for u in (8, 9):
                        for bb in plan[f"ab{u}"]:
                            wait_stored(pe, f"ab{u}", bb)
                slots = prob[:, hd % 2, :]
                for t in range(TB):
                    for j in range(t + 1):
                        mm(bank[bd][:, 400 + t:401 + t],
                           slots[:, t * P:(t + 1) * P] if j == 0 else slots[:, SEQ:SEQ + P], ones_col[:, :],
                           j == 0, j == t)
                values(b, lambda j: tok[:, 2, j, hd * DV:(hd + 1) * DV], slots=slots) \
                    .then_inc(ready[b], 1)

            s_ret(0)
            s_ret(1)
            feature_unit("ab6", unit_no(0, 6), plain)
            y_ret(0)
            y_ret(1)
            s_ret(2)
            s_ret(3)
            feature_unit("ab7", unit_no(0, 7), plain)
            y_ret(2)
            y_ret(3)
            for u in (8, 9):
                token_unit(f"ab{u}", unit_no(0, u))
            y_turn(0, 0)
            y_turn(0, 1)
            s_ml(0)
            s_ml(1)
            token_unit("ab10", unit_no(0, 10))
            y_ml(0)
            y_ml(1)
            s_ml(2)
            s_ml(3)
            token_unit("ab11", unit_no(0, 11))
            y_ml(2)
            y_ml(3)

            def turned(layer, parts):
                for n in parts:
                    for b in plan[f"yturn{layer}_{n}"]:
                        wait_stored(pe, f"yturn{layer}_{n}", b)

            turned(0, (0, 1))
            weights_out(0, 0)
            y_turn(0, 2)
            y_turn(0, 3)
            weights_out(0, 1)
            turned(0, (2, 3))
            weights_out(0, 2)
            weights_out(0, 3)

            def router(layer):
                b = 4
                claim(f"router{layer}", b)
                for t in range(TB):
                    for k in range(KC):
                        last = mm(bank[b][:, t * EXPERTS:(t + 1) * EXPERTS], hT[:, k, t * P:(t + 1) * P],
                                  w_router[:, k, :], k == 0, k == KC - 1)
                last.then_inc(ready[b], 1)

            def experts(w, i, full_at, gathered, layer=None):
                n0 = unit_no(0 if w in passes[0] else 1, LAYER_UNITS)

                def weights(pair, j, k):
                    if layer is not None and pair and j < EARLY:
                        pe.wait_ge(early_in, 32 * EARLY * (layer + 1))
                        return lambda c: early[j][c // (KC // 2)][:, c % (KC // 2), :]
                    n = n0 + 6 * pair + j
                    pe.wait_ge(w.full[n % RING], full_at(n))
                    unit = ring[:, n % RING, :].rearrange("p (k n) -> p k n", k=k)
                    return lambda c: unit[:, c, :]

                def scatter(pair, q):
                    w.read(pe, i, 1, 1 + pair)
                    w.read(pe, i, 2 + q, 2 + 2 * pair)
                    for t in range(TB):
                        last = nc.tensor.matmul(bank[4 + 2 * t + q][:, :], selw_t[:, pair, t * P:(t + 1) * P],
                                                ye[:, q * 512:(q + 1) * 512], start=False, stop=False,
                                                skip_group_check=True)
                    return last

                for b in range(4):
                    w.claim(pe, i, b, 0)
                    mm(bank[b][:, 0:1], ident, ones_col[:, 0:1])
                    for c in range(2):
                        for t in range(TB):
                            last = mm(bank[b][:, c * 2 * ROWS:(c + 1) * 2 * ROWS],
                                      h[:, t, (2 * b + c) * P:(2 * b + c + 1) * P],
                                      sel[:, t, bass.ds(gathered * 4, 4), :], t == 0, t == TB - 1)
                    last.then_inc(w.ready[b], 1)
                for b in range(4):
                    w.read(pe, i, b, 0)
                for pair in range(2):
                    for part in range(2):
                        w.claim(pe, i, 2 + part, 1 + 2 * pair)
                        wt = [weights(pair, 2 * part + e, KC) for e in range(2)]
                        for k in range(KC):
                            for e in range(2):
                                row0 = (2 * pair + e) * BLOCK
                                last = mm(bank[2 + part][e * BLOCK:(e + 1) * BLOCK, :],
                                          xg[:, k, row0:row0 + BLOCK], wt[e](k), k == 0, k == KC - 1)
                        last.then_inc(w.ready[2 + part], 1)
                    w.claim(pe, i, 1, 1 + pair)
                    pe.wait_ge(w.selw, i * 2 + (pair + 1))
                    for t in range(TB):
                        last = nc.tensor.transpose(bank[1][:, t * P:(t + 1) * P], selw[:, t, :], ident)
                    last.then_inc(w.ready[1], 1)
                    if pair and w.main:
                        scatter(0, 0)
                    w.claim(pe, i, 0, 1 + pair)
                    w.read(pe, i, 3, 1 + 2 * pair)
                    for c in range(FF // P):
                        last = nc.tensor.transpose(bank[0][:, c * P:(c + 1) * P], hid[:, c * P:(c + 1) * P], ident)
                    last.then_inc(w.ready[0], 1)
                    if pair and w.main:
                        scatter(0, 1)
                    w.read(pe, i, 0, 1 + pair)
                    for q in range(2):
                        w.claim(pe, i, 2 + q, 2 + 2 * pair)
                        wt = [weights(pair, 4 + e, FF // P) for e in range(2)]
                        for k in range(FF // P):
                            for e in range(2):
                                last = mm(bank[2 + q][e * BLOCK:(e + 1) * BLOCK, :],
                                          hid_t[:, k, e * BLOCK:(e + 1) * BLOCK],
                                          wt[e](k)[:, q * 512:(q + 1) * 512], k == 0, k == FF // P - 1)
                        last.then_inc(w.ready[2 + q], 1)
                    if pair or not w.main:
                        for q in range(2):
                            last = scatter(pair, q)
                        if not w.main:
                            last.then_inc(w.slots, 1)

            def moe(layer):
                turn_h(f"mix_turn{layer}_", TB * 2 * layer)
                wait_hT(f"mix_turn{layer}_")
                router(layer)
                def zero(b):
                    claim(f"ffn{layer}", b)
                    nc.tensor.matmul(bank[b][:, :], zero_row[0:1, :], consts[0:1, 0:512], start=True, stop=False,
                                     skip_group_check=True)

                for b in range(5, 8):
                    zero(b)
                claim(f"rank{layer}", 4)
                pe.wait_ge(rank_in, layer + 1)
                upto, all_ones = cmask[:, 0:P], cmask[:, P:2 * P]
                picks = route[:, 2, :, :]
                mm(bank[4][:, 0:EXPERTS], upto, picks[:, 0, :])
                mm(bank[4][:, EXPERTS:2 * EXPERTS], all_ones, picks[:, 0, :], True, False)
                mm(bank[4][:, EXPERTS:2 * EXPERTS], upto, picks[:, 1, :], False, True)
                mm(bank[4][:, 2 * EXPERTS:3 * EXPERTS], all_ones, picks[:, 0, :], True, False)
                mm(bank[4][:, 2 * EXPERTS:3 * EXPERTS], all_ones, picks[:, 1, :], False, True) \
                    .then_inc(ready[4], 1)
                pe.wait_ge(load_ready, layer + 1)
                load = pe.value_load(load_i[0:1, 0:1], min_val=0, max_val=SEQ)
                zero(4)
                first, more = passes[layer]
                pe.wait_ge(first.sel, 1)
                with pe.Fori(0, QUADS - 1) as i:
                    experts(first, i, lambda n: i * 32 + landed(n), i)
                experts(first, QUADS - 1, lambda n: (QUADS - 1) * 32 + landed(n), QUADS - 1, layer)
                with pe.If(load > BLOCK):
                    nc.tensor.matmul(bank[4][:, :], zero_row[0:1, :], consts[0:1, 0:512], start=False, stop=False,
                                     skip_group_check=True).then_inc(more.slots, 1)
                    with pe.Fori(0, PASSES - 1) as p:
                        pe.wait_ge(more.sel, p + 1)
                        nc.tensor.matmul(bank[4][:, :], zero_row[0:1, :], consts[0:1, 0:512], start=False,
                                         stop=False, skip_group_check=True)
                        with pe.Fori(0, QUADS) as i:
                            at = p * QUADS + i
                            n0 = unit_no(layer, LAYER_UNITS)
                            experts(more, at, lambda n: at * 32 + (16 + 16 * ((n - n0) // RING)), i)
                for b in range(4, 8):
                    nc.tensor.matmul(bank[b][:, :], zero_row[0:1, :], consts[0:1, 0:512], start=False, stop=True,
                                     skip_group_check=True).then_inc(ready[b], 1)

            moe(0)

            turn_h("ffn_turn0_", TB)
            wait_hT("ffn_turn0_")
            for u in range(2):
                feature_unit(f"cd{u}", unit_no(1, u), plain)
            b0, b1 = plan["alpha_in"]
            claim("alpha_in", b0)
            claim("alpha_in", b1)
            for b, w in ((b0, tail_a), (b1, tail_dt)):
                for k in range(KC):
                    last = mm(bank[b][0:16, 0:SEQ], w[:, k, :], hT[:, k, :], k == 0, k == KC - 1)
                last.then_inc(ready[b], 1)
            wait_stored(pe, "alpha_in", b0)
            for q, b in enumerate(plan["alpha"]):
                claim("alpha", b)
                for hd in (2 * q, 2 * q + 1):
                    last = mm(bank[b][:, (hd % 2) * SEQ:(hd % 2 + 1) * SEQ], w_alpha[:, hd * DK:(hd + 1) * DK],
                              gate_row[0:16, 0, :])
                last.then_inc(ready[b], 1)
            b0 = first_of("dt_cols")
            claim("dt_cols", b0)
            pe.wait_ge(gate_ok, 2)
            for q, row in enumerate((2, 3)):
                for t in range(TB):
                    last = nc.tensor.transpose(bank[b0][:, (q * TB + t) * 16:(q * TB + t + 1) * 16],
                                               gate_row[0:16, row, t * P:(t + 1) * P],
                                               consts[0:16, C_ID:C_ID + 16])
            last.then_inc(ready[b0], 1)
            for u in range(2, 6):
                token_unit(f"cd{u}", unit_no(1, u))

            def s_gla(hd):
                b = first_of(f"s_gla{hd}")
                claim(f"s_gla{hd}", b)
                for i in range(SEQ // GLA_BLOCK):
                    pe.wait_ge(kscale, 8 * hd + i + 1)
                    cols = slice(i * GLA_BLOCK, (i + 1) * GLA_BLOCK)
                    kk = gtmp[:, i % 2, :]
                    for j in range(2 if i >= 4 else 1):
                        last = mm(bank[b][:, j * P + cols.start:j * P + cols.stop], kk[:, j * P:(j + 1) * P],
                                  feat[:, hd, cols])
                    if i < SEQ // GLA_BLOCK - 1:
                        last.then_inc(kused, 1)
                last.then_inc(ready[b], 1)

            def y_gla(hd):
                b = first_of(f"y_gla{hd}")
                claim(f"y_gla{hd}", b)
                wait_stored(pe, f"s_gla{hd}", first_of(f"s_gla{hd}"))
                if hd == 0:
                    for u in (2, 3):
                        for bb in plan[f"cd{u}"]:
                            wait_stored(pe, f"cd{u}", bb)
                values(b, lambda j: tok[:, 0, j, hd * DV:(hd + 1) * DV],
                       slots=prob[:, hd % 2, :]).then_inc(ready[b], 1)

            s_gla(0)
            s_gla(1)
            feature_unit("cd6", unit_no(1, 6), plain)
            y_gla(0)
            y_gla(1)
            feature_unit("cd7", unit_no(1, 7), plain)
            s_gla(2)
            s_gla(3)
            feature_unit("cd8", unit_no(1, 8), plain)
            y_gla(2)
            y_gla(3)
            feature_unit("cd9", unit_no(1, 9), plain)
            for u in (10, 11):
                token_unit(f"cd{u}", unit_no(1, u))
            y_turn(1, 0)
            y_turn(1, 1)
            for u in range(6, 10):
                for bb in plan[f"cd{u}"]:
                    wait_stored(pe, f"cd{u}", bb)
            for n in range(4):
                for q, b in enumerate(plan[f"xs_turn{n}"]):
                    claim(f"xs_turn{n}", b)
                    t, c0 = n // 2, 4 * (n % 2) + 2 * q
                    for c in range(2):
                        last = nc.tensor.transpose(bank[b][:, c * P:(c + 1) * P],
                                                   feat[:, 8 + c0 + c, t * P:(t + 1) * P], ident)
                    last.then_inc(ready[b], 1)
            for g in range(GROUPS):
                for q, b in enumerate(plan[f"cum{g}"]):
                    claim(f"cum{g}", b)
                    for r in (2 * q, 2 * q + 1):
                        hd = 4 * g + r
                        last = mm(bank[b][:, (r % 2) * SEQ:(r % 2 + 1) * SEQ],
                                  consts[0:16, C_ID + hd:C_ID + hd + 1].to_broadcast([16, P]),
                                  gate_row[0:16, 3, :])
                    last.then_inc(ready[b], 1)
                b = first_of(f"s_ssd{g}")
                claim(f"s_ssd{g}", b)
                score_group(b, feat[:, 16 + g, :], feat[:, 20 + g, :], full).then_inc(ready[b], 1)
                if g == 1:
                    turned(1, (0, 1))
                if g:
                    weights_out(1, (g - 1) // TB, ((g - 1) % TB,))
                b = first_of(f"y_ssd{g}")
                claim(f"y_ssd{g}", b)
                if g == 0:
                    for n in range(4):
                        for bb in plan[f"xs_turn{n}"]:
                            wait_stored(pe, f"xs_turn{n}", bb)
                for r in range(4):
                    hd = 4 * g + r
                    if r < 3:
                        pe.wait_ge(prob_ready, HEADS + 3 * g + r + 1)
                    else:
                        wait_stored(pe, f"s_ssd{g}", first_of(f"s_ssd{g}"))
                    last = values(b, lambda j: xdt[:, j, hd * SSD_HD:(hd + 1) * SSD_HD],
                                  start_cols=r * SSD_HD, width=SSD_HD, slots=prob[:, hd % 2, :])
                    if r < 3:
                        last.then_inc(kused, 1)
                last.then_inc(ready[b], 1)
            y_turn(1, 2)
            weights_out(1, 1, (1,))
            y_turn(1, 3)
            turned(1, (2, 3))
            weights_out(1, 2)
            weights_out(1, 3)
            moe(1)

        @block.scalar
        def _(act):
            steps = [0]
            roots = [0]

            def step(ins):
                ins.then_inc(act_step, 1)
                steps[0] += 1

            def settle():
                act.wait_ge(act_step, steps[0])

            def fn(o, i, f, **kw):
                return nc.scalar.activation(o, i, f, **kw)

            def copy_turn(name, q, dst):
                b = list(plan[name])[q]
                wait_ready(act, name, b)
                nc.scalar.copy(dst, bank[b][:, :]).then_inc(stored[b], 1)

            def turn_h(tag):
                for j in range(2):
                    copy_turn(f"{tag}{j}", 1, hT[:, 4 * j + 2:4 * j + 4, :].rearrange("p k t -> p (k t)"))

            def token_unit(name, f):
                i, half = tok_sets[name]
                for t, b in enumerate(plan[name]):
                    wait_ready(act, name, b)
                    fn(tok[:, i, t, half * 512:(half + 1) * 512], bank[b][:, :], f).then_inc(stored[b], 1)

            def root(e, src, t=None):
                roots[0] += 1
                act.preload_act_table_set("natural_log_exp_and_others")
                act.wait_ge(var_ready, roots[0])
                r = slice(0, TB) if t is None else slice(t, t + 1)
                step(fn(rstd[:, r], src[:, r], ACT.Ln, bias=eps[:, e:e + 1]))
                settle()
                fn(rstd[:, r], rstd[:, r], ACT.Exp, scale=-0.5).then_inc(rstd_ready, 1)

            def y_turns(layer, cols, parts):
                for n in parts:
                    b = list(plan[f"yturn{layer}_{n}"])[1]
                    wait_ready(act, f"yturn{layer}_{n}", b)
                    for k in range(2):
                        c = 4 * n + 2 + k
                        ins = fn(yT[:, c, :], bank[b][:, k * SEQ:(k + 1) * SEQ], ACT.Copy, scale=cols[:, c:c + 1])
                        step(ins) if k == 0 else ins.then_inc(stored[b], 1)

            def conv_unit(name, first, cols, w0, b0, tile0, n_done):
                for m in range(4):
                    b = list(plan[name])[m // 2]
                    wait_ready(act, name, b)
                    fn(feat[:, first + m, :], bank[b][:, (m % 2) * SEQ:(m % 2 + 1) * SEQ], ACT.Identity,
                       scale=cols[:, w0 + tile0 + m:w0 + tile0 + m + 1],
                       bias=cols[:, b0 + tile0 + m:b0 + tile0 + m + 1]).then_inc(conv_first, 1)
                    act.wait_ge(conv_sum, n_done + m + 1)
                    ins = fn(feat[:, first + m, :], feat[:, first + m, :], ACT.Silu)
                    if m % 2:
                        ins.then_inc(stored[b], 1)

            act.wait_ge(dve_step, 5)
            act.wait_ge(par_in, 16 * PAR_FIRST)
            turn_h("x_turn")
            act.wait_ge(trig_arg, 1)
            fn(trig[:, 0, 0:SEQ], turns[:, 0, :], ACT.Sin).then_inc(trig_done, 1)
            fn(trig[:, 0, SEQ:512], turns[:, 1, :], ACT.Sin).then_inc(trig_done, 1)
            act.wait_ge(gate_a, 1)
            step(fn(gate_row[0:HEADS, 1, :], gate_row[0:HEADS, 1, :], ACT.Exp, scale=-1.0))
            settle()
            fn(gate_row[0:HEADS, 1, :], gate_row[0:HEADS, 1, :], ACT.Ln, bias=1.0).then_inc(gate_b, 1)
            act.wait_ge(gate_a, 2)
            fn(gate_row[0:HEADS, 4, :], gate_row[0:HEADS, 4, :], ACT.Exp, scale=-1.0).then_inc(gate_ok, 1)
            for u in (2, 3):
                token_unit(f"ab{u}", ACT.Copy)
            for u in (4, 5):
                token_unit(f"ab{u}", ACT.Silu)
            act.wait_ge(rot_ready, 4)
            for hd in range(HEADS):
                fn(dec[:, hd, :], dist, ACT.Exp, scale=LOG_GAMMA[hd]).then_inc(dec_done, 1)
            root(1, mv[:, :, 1])
            root(1, mv[:, :, 1])
            conv_unit("ab6", 8, cols_ab, ROWS_AB["conv_w"] + 24, ROWS_AB["conv_b"], 0, 0)
            root(1, mv[:, :, 1])
            root(1, mv[:, :, 1])
            conv_unit("ab7", 12, cols_ab, ROWS_AB["conv_w"] + 24, ROWS_AB["conv_b"], 4, 4)
            for u in (8, 9):
                token_unit(f"ab{u}", ACT.Copy)
            wait_stored(act, "s_ret3", first_of("s_ret3"))
            y_turns(0, cols_ab, (0, 1))
            for b in plan["gate_rows"]:
                wait_stored(act, "gate_rows", b)
            for hd in range(HEADS):
                fn(mlexp[:, hd, :], mlexp[:, hd, :], ACT.Exp).then_inc(dec_done, 1)
            token_unit("ab10", ACT.Sigmoid)
            root(1, mv[:, :, 1])
            root(1, mv[:, :, 1])
            token_unit("ab11", ACT.Sigmoid)
            root(1, mv[:, :, 1])
            root(1, mv[:, :, 1])

            y_turns(0, cols_ab, (2, 3))
            for t in range(TB):
                root(0, mv[:, :, 1], t)

            def moe(layer):
                turn_h(f"mix_turn{layer}_")
                wait_stored(act, f"router{layer}", 4)
                fn(route[:, 0, :, :], route[:, 0, :, :], ACT.Exp).then_inc(r_exp, 1)
                act.wait_ge(load_ready, layer + 1)
                load = act.value_load(load_i[0:1, 0:1], min_val=0, max_val=SEQ)
                first, more = passes[layer]

                def experts(w, i):
                    for b in (0, 2):
                        w.filled(act, i, b, 0)
                        fn(flat(xg[:, 2 * b:2 * b + 2, :]), bank[b][:, :], ACT.Copy).then_inc(w.stored[b], 1)
                    for pair in range(2):
                        w.filled(act, i, 2, 1 + 2 * pair)
                        fn(sil, bank[2][:, :], ACT.Silu).then_inc(w.stored[2], 1)
                        w.filled(act, i, 0, 1 + pair)
                        fn(flat(hid_t), bank[0][:, :], ACT.Copy).then_inc(w.stored[0], 1)
                        w.filled(act, i, 2, 2 + 2 * pair)
                        fn(ye[:, 0:512], bank[2][:, :], ACT.Copy).then_inc(w.stored[2], 1)

                act.preload_act_table_set("silu_and_others")
                with act.Fori(0, QUADS) as i:
                    experts(first, i)
                with act.If(load > BLOCK):
                    with act.Fori(0, PASSES - 1) as p:
                        with act.Fori(0, QUADS) as i:
                            experts(more, p * QUADS + i)
                for t in range(TB):
                    root(0, mv[:, :, 1], t)

            moe(0)
            turn_h("ffn_turn0_")

            act.wait_ge(par_late, 16 * (len(par_list) - PAR_FIRST))
            act.wait_ge(gate_a, 3)
            step(fn(gate_row[0:16, 2, :], gate_row[0:16, 1, :], ACT.Exp, scale=-1.0))
            settle()
            step(fn(gate_row[0:16, 2, :], gate_row[0:16, 2, :], ACT.Ln, bias=1.0))
            fn(ssd_par[:, 1:2], ssd_par[:, 1:2], ACT.Exp).then_inc(gate_b, 1)
            act.wait_ge(gate_a, 4)
            step(fn(flat(gtmp), flat(gtmp), ACT.Exp, scale=-1.0))
            settle()
            fn(flat(gtmp), flat(gtmp), ACT.Ln, bias=1.0).then_inc(gate_b, 1)
            for u in (2, 3):
                token_unit(f"cd{u}", ACT.Copy)
            for u in (4, 5):
                token_unit(f"cd{u}", ACT.Silu)

            def gla_head(hd):
                act.wait_ge(dec_arg, hd + 1)
                fn(dec[:, hd, 0:SEQ], dec[:, hd, 0:SEQ], ACT.Exp, scale=1.0 / GLA_TAU).then_inc(dec_done, 1)
                for i in range(SEQ // GLA_BLOCK):
                    n = P if i < 4 else SEQ
                    k = 8 * hd + i
                    if k >= 2:
                        act.wait_ge(kscale, k - 1)
                    fn(gtmp[:, 2 + i % 2, 0:n], bcum[:, hd, 0:n], ACT.Exp, scale=-1.0 / GLA_TAU,
                       bias=gate_col[:, 0, :, :].rearrange("p a b -> p (a b)")[:, k:k + 1]).then_inc(kexp, 1)

            act.wait_ge(gate_a, 5)
            gla_head(0)
            gla_head(1)
            root(1, mv[:, :, 1])
            root(1, mv[:, :, 1])
            conv_unit("cd6", 8, cols_cd, ROWS_CD["conv_w"] + 48, ROWS_CD["conv_b"], 0, 8)
            gla_head(2)
            gla_head(3)
            conv_unit("cd7", 12, cols_cd, ROWS_CD["conv_w"] + 48, ROWS_CD["conv_b"], 4, 12)
            root(1, mv[:, :, 1])
            root(1, mv[:, :, 1])
            conv_unit("cd8", 16, cols_cd, ROWS_CD["conv_w"] + 48, ROWS_CD["conv_b"], 8, 16)
            conv_unit("cd9", 20, cols_cd, ROWS_CD["conv_w"] + 48, ROWS_CD["conv_b"], 12, 20)
            for u in (10, 11):
                token_unit(f"cd{u}", ACT.Silu)
            y_turns(1, cols_cd, (0, 1))
            act.preload_act_table_set("natural_log_exp_and_others")
            for g in range(GROUPS):
                for r in range(4):
                    if r % 2:
                        b = list(plan[f"cum{g}"])[r // 2]
                        wait_stored(act, f"cum{g}", b)
                    else:
                        act.wait_ge(dec_arg, HEADS + 2 * g + r // 2 + 1)
                    fn(ssd_dec[:, r, :], ssd_dec[:, r, :], ACT.Exp).then_inc(dec_done, 1)
                root(1, mv[:, :, 1])
            y_turns(1, cols_cd, (2, 3))
            for t in range(TB):
                root(0, mv[:, :, 1], t)
            moe(1)

        @block.vector
        def _(dve):
            V = nc.vector
            steps = [0]
            roots = [0]
            lns = [0]

            def step(ins):
                ins.then_inc(dve_step, 1)
                steps[0] += 1

            def settle():
                dve.wait_ge(dve_step, steps[0])

            def link(ins):
                step(ins)
                settle()

            def turn_h(tag):
                for j in range(2):
                    name = f"{tag}{j}"
                    b = list(plan[name])[0]
                    wait_ready(dve, name, b)
                    V.tensor_copy(hT[:, 4 * j:4 * j + 2, :].rearrange("p k t -> p (k t)"), bank[b][:, :]) \
                        .then_inc(stored[b], 1)

            step(V.memset(ones_row[:, :], 1.0))
            step(V.memset(ones_col[:, :], 1.0))
            step(V.memset(gate_col[:, :, :, :], 0.0))
            step(V.memset(eps[:, 0:1], LN_EPS))
            step(V.memset(eps[:, 1:2], NORM_EPS))
            step(V.memset(zero_row[:, :], 0.0))
            dve.wait_ge(par_in, 16 * PAR_FIRST)
            turn_h("x_turn")
            for (dst, n), b in zip(((cols_ab, ROWS_AB["n"]), (cols_cd, ROWS_CD["n"])), plan["params"]):
                wait_ready(dve, "params", b)
                V.tensor_copy(dst[:, :], bank[b][:, 0:n]).then_inc(stored[b], 1)
            link(V.tensor_copy(pos_f, pos_i))
            link(V.tensor_scalar(angle, pos_f, consts[:, C_FREQ:C_FREQ + 1], None, ALU.mult))
            for q, shift in enumerate((0.25, 0.0)):
                link(V.tensor_scalar(turns[:, q, :], angle, 1.0 / TWO_PI, shift, ALU.mult, ALU.add))
                link(V.tensor_scalar(turns[:, q, :], turns[:, q, :], ROUND, None, ALU.add))
                link(V.tensor_scalar(turns[:, q, :], turns[:, q, :], -ROUND, None, ALU.add))
                link(V.scalar_tensor_tensor(out=pos_f, in0=turns[:, q, :], scalar=-PI_A, in1=angle,
                                            op0=ALU.mult, op1=ALU.add))
                link(V.scalar_tensor_tensor(out=pos_f, in0=turns[:, q, :], scalar=-PI_B, in1=pos_f,
                                            op0=ALU.mult, op1=ALU.add))
                link(V.scalar_tensor_tensor(out=turns[:, q, :], in0=turns[:, q, :], scalar=-PI_C, in1=pos_f,
                                            op0=ALU.mult, op1=ALU.add))
                link(V.tensor_scalar(turns[:, q, :], turns[:, q, :], float(TWO_PI * shift), PI_SAFE, ALU.add,
                                     ALU.min))
                ins = V.tensor_scalar(turns[:, q, :], turns[:, q, :], -PI_SAFE, None, ALU.max)
                if q == 0:
                    link(ins)
                else:
                    ins.then_inc(trig_arg, 1)
            dve.wait_ge(trig_done, 2)
            step(V.tensor_scalar(trig[:, 1, 0:SEQ], trig[:, 0, SEQ:512], -1.0, None, ALU.mult))
            link(V.tensor_copy(trig[:, 1, SEQ:512], trig[:, 0, 0:SEQ]))

            def rotate(name, first):
                for q, b in enumerate(plan[name]):
                    wait_ready(dve, name, b)
                    even = bank[b][:, 0:SEQ].rearrange("p (o t) -> p o t", o=1).to_broadcast([P, 2, SEQ])
                    odd = bank[b][:, SEQ:512].rearrange("p (o t) -> p o t", o=1).to_broadcast([P, 2, SEQ])
                    two = lambda x: x.rearrange("p (c t) -> p c t", c=2)
                    if q or name == "ab1":
                        dve.wait_ge(rot_ready, q + 2 * (name == "ab1"))
                    step(V.tensor_tensor(two(rot[:, 0, :]), even, two(trig[:, 0, :]), ALU.mult))
                    V.tensor_tensor(two(rot[:, 1, :]), odd, two(trig[:, 1, :]), ALU.mult).then_inc(stored[b], 1)
                    settle()
                    wait_stored(dve, name, b)
                    V.tensor_tensor(feat[:, first + 2 * q:first + 2 * q + 2, :], two(rot[:, 0, :]),
                                    two(rot[:, 1, :]), ALU.add).then_inc(rot_ready, 1)

            rotate("ab0", 0)
            rotate("ab1", 4)

            dve.wait_ge(par_late, 16 * (len(par_list) - PAR_FIRST))
            b0 = first_of("gates")
            wait_ready(dve, "gates", b0)
            G = gate_row[0:HEADS, :, :]
            link(V.tensor_scalar(G[:, 0, :], bank[b0][0:HEADS, SEQ:512], ml_bias[:, 1:2], None, ALU.add))
            V.tensor_scalar(G[:, 2, :], bank[b0][0:HEADS, 0:SEQ], ml_bias[:, 0:1], None, ALU.add) \
                .then_inc(stored[b0], 1)
            V.scalar_tensor_tensor(out=G[:, 1, :], in0=G[:, 0, :], scalar=-1.0, in1=G[:, 0, :], op0=ALU.mult,
                                   op1=ALU.max).then_inc(gate_a, 1)
            dve.wait_ge(gate_b, 1)
            link(V.scalar_tensor_tensor(out=G[:, 0, :], in0=G[:, 0, :], scalar=0.0, in1=G[:, 1, :],
                                        op0=ALU.min, op1=ALU.subtract))
            link(V.tensor_tensor_scan(G[:, 1, :], ones_row[0:HEADS, :], G[:, 0, :], 0.0, ALU.mult, ALU.add))
            link(V.tensor_tensor(G[:, 2, :], G[:, 2, :], G[:, 1, :], ALU.subtract))
            link(V.tensor_tensor_scan(G[:, 3, :], ones_row[0:HEADS, :], G[:, 2, :], 0.0, ALU.mult, ALU.max))
            link(V.tensor_tensor(G[:, 4, :], G[:, 1, :], G[:, 3, :], ALU.add))
            V.tensor_scalar(G[:, 3, :], G[:, 3, :], -1.0, None, ALU.mult).then_inc(gate_a, 1)
            b0 = first_of("gate_cols")
            wait_ready(dve, "gate_cols", b0)
            V.tensor_copy(gate_col[:, :, :, 0:HEADS],
                          bank[b0][:, 0:64].rearrange("p (q t n) -> p q t n", q=2, t=TB)[:, :, :, 0:HEADS]) \
                .then_inc(stored[b0], 1)
            wait_stored(dve, "gate_cols", b0)

            def decay_args(name, heads, buf, n0):
                for q, b in enumerate(plan[name]):
                    wait_ready(dve, name, b)
                    for r in (2 * q, 2 * q + 1):
                        for j in range(2):
                            ins = V.scalar_tensor_tensor(
                                out=buf(r)[:, j * SEQ:j * SEQ + SEQ - j * P],
                                in0=bank[b][:, (r % 2) * SEQ + j * P:(r % 2 + 1) * SEQ],
                                scalar=heads(r, j), in1=cap[:, j * SEQ:j * SEQ + SEQ - j * P],
                                op0=ALU.add, op1=ALU.min)
                            if j == 0:
                                step(ins)
                            else:
                                ins.then_inc(stored[b] if r % 2 else dec_arg, 1)

            for q, b in enumerate(plan["gate_rows"]):
                wait_ready(dve, "gate_rows", b)
                for r in (2 * q, 2 * q + 1):
                    for j in range(2):
                        ins = (V.scalar_tensor_tensor(
                            out=mlexp[:, r, j * SEQ:j * SEQ + SEQ - j * P],
                            in0=bank[b][:, (r % 2) * SEQ + j * P:(r % 2 + 1) * SEQ],
                            scalar=gate_col[:, 0, j, r:r + 1], in1=cap[:, j * SEQ:j * SEQ + SEQ - j * P],
                            op0=ALU.add, op1=ALU.min))
                        step(ins) if not (r % 2 and j) else ins.then_inc(stored[b], 1)

            def head_stats(src):
                for t in range(TB):
                    step(V.bn_stats(stat[:, t, :], src(t)))
                settle()
                step(V.bn_aggr(mv[:, 0, :], stat[:, 0, :]))
                V.bn_aggr(mv[:, 1, :], stat[:, 1, :]).then_inc(var_ready, 1)

            def wait_root():
                roots[0] += 1
                dve.wait_ge(rstd_ready, roots[0])
                dve.wait_ge(var_ready, roots[0])

            def decayed(s_name, b, n_prob, scale, factor, n_dec):
                wait_ready(dve, s_name, b)
                dve.wait_ge(dec_done, n_dec) if n_dec else None
                return V.scalar_tensor_tensor(out=prob[:, n_prob % 2, :], in0=bank[b][:, 0:CAUSAL], scalar=scale,
                                              in1=factor, op0=ALU.mult, op1=ALU.mult)

            def p_ret(hd):
                b = first_of(f"s_ret{hd}")
                decayed(f"s_ret{hd}", b, hd, QK_SCALE, dec[:, hd, :], hd + 1).then_inc(stored[b], 1)

            def y_ret(hd):
                b = first_of(f"y_ret{hd}")
                wait_ready(dve, f"y_ret{hd}", b)
                head_stats(lambda t: bank[b][:, t * DV:(t + 1) * DV])
                wait_root()
                cols = slice(hd * DV, (hd + 1) * DV)
                for u in (4, 5):
                    for bb in plan[f"ab{u}"]:
                        wait_stored(dve, f"ab{u}", bb)
                for t in range(TB):
                    ins = V.scalar_tensor_tensor(out=tok[:, 1, t, cols], in0=bank[b][:, t * DV:(t + 1) * DV],
                                                 scalar=mv[:, t, 0:1], in1=tok[:, 1, t, cols],
                                                 op0=ALU.subtract, op1=ALU.mult)
                    ins.then_inc(stored[b], 1) if t else step(ins)
                wait_stored(dve, f"y_ret{hd}", b)
                for t in range(TB):
                    ins = V.tensor_scalar(tok[:, 1, t, cols], tok[:, 1, t, cols], rstd[:, t:t + 1], None, ALU.mult)
                    link(ins) if t == 0 else ins.then_inc(y_done, 1)
                dve.wait_ge(y_done, hd + 1)

            p_ret(0)
            p_ret(1)
            y_ret(0)
            y_ret(1)

            def taps(name, first, cols, w0, n_tiles, tile0, n_done):
                for m in range(4):
                    b = list(plan[name])[m // 2]
                    dve.wait_ge(conv_first, n_done + m + 1)
                    for back in (1, 2, 3):
                        o = feat[:, first + m, back:SEQ]
                        c = w0 + (3 - back) * n_tiles + tile0 + m
                        ins = V.scalar_tensor_tensor(
                            out=o, in0=bank[b][:, (m % 2) * SEQ:(m % 2 + 1) * SEQ - back],
                            scalar=cols[:, c:c + 1], in1=o, op0=ALU.mult, op1=ALU.add)
                        link(ins) if back < 3 else ins.then_inc(conv_sum, 1)

            taps("ab6", 8, cols_ab, ROWS_AB["conv_w"], 8, 0, 0)
            p_ret(2)
            p_ret(3)
            y_ret(2)
            y_ret(3)
            taps("ab7", 12, cols_ab, ROWS_AB["conv_w"], 8, 4, 4)

            def y_turns(layer, cols, parts):
                for n in parts:
                    b = list(plan[f"yturn{layer}_{n}"])[0]
                    wait_ready(dve, f"yturn{layer}_{n}", b)
                    for k in range(2):
                        c = 4 * n + k
                        ins = V.tensor_scalar(yT[:, c, :], bank[b][:, k * SEQ:(k + 1) * SEQ], cols[:, c:c + 1], None,
                                              ALU.mult)
                        step(ins) if k == 0 else ins.then_inc(stored[b], 1)

            y_turns(0, cols_ab, (0, 1))

            def p_ml(hd):
                b = first_of(f"s_ml{hd}")
                decayed(f"s_ml{hd}", b, hd, QK_SCALE, mlexp[:, hd, :], 4 + hd + 1).then_inc(prob_ready, 1)

            def y_ml(hd):
                b, bd = first_of(f"y_ml{hd}"), first_of(f"s_ml{hd}")
                wait_ready(dve, f"y_ml{hd}", b)
                V.tensor_copy(rec[:, :], bank[bd][:, 400:402]).then_inc(stored[bd], 1)
                wait_stored(dve, f"s_ml{hd}", bd)
                link(V.scalar_tensor_tensor(out=rec[:, :], in0=rec[:, :], scalar=-1.0, in1=rec[:, :], op0=ALU.mult,
                                            op1=ALU.max))
                link(V.tensor_tensor(rec[:, :], rec[:, :], gate_col[:, 1, :, hd], ALU.max))
                link(V.reciprocal(rec[:, :], rec[:, :]))
                cols = slice(hd * DV, (hd + 1) * DV)
                for bb in plan["ab10" if hd < 2 else "ab11"]:
                    wait_stored(dve, "ab10" if hd < 2 else "ab11", bb)
                for t in range(TB):
                    ins = V.scalar_tensor_tensor(out=tok[:, 3, t, cols], in0=bank[b][:, t * DV:(t + 1) * DV],
                                                 scalar=rec[:, t:t + 1], in1=tok[:, 3, t, cols],
                                                 op0=ALU.mult, op1=ALU.mult)
                    ins.then_inc(stored[b], 1) if t else step(ins)
                wait_stored(dve, f"y_ml{hd}", b)
                head_stats(lambda t: tok[:, 3, t, cols])
                wait_root()
                for t in range(TB):
                    ins = V.tensor_scalar(tok[:, 3, t, cols], tok[:, 3, t, cols], mv[:, t, 0:1], rstd[:, t:t + 1],
                                          ALU.subtract, ALU.mult)
                    link(ins) if t == 0 else ins.then_inc(y_done, 1)
                dve.wait_ge(y_done, 4 + hd + 1)

            p_ml(0)
            p_ml(1)
            y_ml(0)
            y_ml(1)
            p_ml(2)
            p_ml(3)
            y_ml(2)
            y_ml(3)

            def layernorm(add, n_ready):
                layer, after_ffn = divmod(n_ready // TB, 2)
                dve.wait_ge(ln_ffn_in if after_ffn else ln_in, 32 * (layer + 1))
                for t in range(TB):
                    for half in range(2):
                        add(t, half)
                        step(V.bn_stats(stat[:, 2 * t + half, :], h[:, t, half * 512:(half + 1) * 512]))
                    settle()
                    V.bn_aggr(mv[:, t, :], stat[:, 2 * t:2 * t + 2, :]).then_inc(var_ready, 1)
                    wait_root()
                    link(V.scalar_tensor_tensor(out=h[:, t, :], in0=h[:, t, :], scalar=mv[:, t, 0:1],
                                                in1=lnp[:, 0, :], op0=ALU.subtract, op1=ALU.mult))
                    V.scalar_tensor_tensor(out=h[:, t, :], in0=h[:, t, :], scalar=rstd[:, t:t + 1],
                                           in1=lnp[:, 1, :], op0=ALU.mult, op1=ALU.add).then_inc(h_ready, 1)

            def add_mix(layer):
                def add(t, half):
                    b = 2 * t + half
                    wait_ready(dve, f"mix{layer}", b)
                    V.scalar_tensor_tensor(out=h[:, t, half * 512:(half + 1) * 512],
                                           in0=h[:, t, half * 512:(half + 1) * 512], scalar=ALPHA,
                                           in1=bank[b][:, :], op0=ALU.mult, op1=ALU.add).then_inc(stored[b], 1)
                    wait_stored(dve, f"mix{layer}", b)
                return add

            y_turns(0, cols_ab, (2, 3))
            layernorm(add_mix(0), 0)

            def routing(layer):
                b = 4
                name = f"router{layer}"
                wait_ready(dve, name, b)
                R = route
                logits = bank[b][:, 0:TB * EXPERTS].rearrange("p (t e) -> p t e", t=TB)
                wide = lambda x: x.rearrange("p (t o) -> p t o", o=1).to_broadcast([P, TB, EXPERTS])
                mx, sm = rstd[:, :], rec[:, :]
                grp = lambda x: x.rearrange("p t (g e) -> p t g e", g=GROUPS)
                link(V.tensor_reduce(mx, logits, AX.X, ALU.max))
                V.tensor_tensor(R[:, 0, :, :], logits, wide(mx), ALU.subtract).then_inc(stored[b], 1)
                dve.wait_ge(r_exp, layer + 1)
                link(V.tensor_reduce(sm, R[:, 0, :, :], AX.X, ALU.add))
                link(V.reciprocal(sm, sm))
                link(V.tensor_tensor(R[:, 0, :, :], R[:, 0, :, :], wide(sm), ALU.mult))
                link(V.tensor_tensor(R[:, 1, :, :], R[:, 0, :, :], b_router[:, :, :], ALU.add))
                s = grp(R[:, 1, :, :])
                S = lambda i: rsmall[:, i, :, :]
                m = [s[:, :, :, i] for i in range(PER_GROUP)]
                link(V.tensor_tensor(S(0), m[0], m[1], ALU.max))
                link(V.tensor_tensor(S(1), m[0], m[1], ALU.min))
                link(V.tensor_tensor(S(2), m[2], m[3], ALU.max))
                link(V.tensor_tensor(S(3), m[2], m[3], ALU.min))
                link(V.tensor_tensor(S(4), S(0), S(2), ALU.max))
                link(V.tensor_tensor(S(5), S(0), S(2), ALU.min))
                link(V.tensor_tensor(S(1), S(1), S(3), ALU.max))
                link(V.tensor_tensor(S(1), S(1), S(5), ALU.max))
                link(V.tensor_tensor(S(4), S(4), S(1), ALU.add))
                narrow = lambda x: x.rearrange("p (t o) -> p t o", o=1).to_broadcast([P, TB, GROUPS])
                order4 = pri[:, EXPERTS - GROUPS:EXPERTS].rearrange("p (o e) -> p o e", o=1) \
                    .to_broadcast([P, TB, GROUPS])
                order16 = pri.rearrange("p (o e) -> p o e", o=1).to_broadcast([P, TB, EXPERTS])
                link(V.tensor_reduce(mx, S(4), AX.X, ALU.max))
                link(V.tensor_tensor(S(0), S(4), narrow(mx), ALU.is_equal))
                link(V.tensor_tensor(S(0), S(0), order4, ALU.mult))
                link(V.tensor_reduce(mx, S(0), AX.X, ALU.max))
                link(V.tensor_tensor(S(0), S(0), narrow(mx), ALU.is_equal))
                link(V.tensor_scalar(S(0), S(0), 1e30, -1e30, ALU.mult, ALU.add))
                for t in range(TB):
                    in_group = rsmall[:, 0, t, :].rearrange("p (g o) -> p g o", o=1) \
                        .to_broadcast([P, GROUPS, PER_GROUP])
                    link(V.tensor_tensor(R[:, 1, t, :].rearrange("p (g e) -> p g e", g=GROUPS),
                                         R[:, 1, t, :].rearrange("p (g e) -> p g e", g=GROUPS), in_group, ALU.add))
                for pick in (2, 3):
                    link(V.tensor_reduce(mx, R[:, 1, :, :], AX.X, ALU.max))
                    link(V.tensor_tensor(R[:, pick, :, :], R[:, 1, :, :], wide(mx), ALU.is_equal))
                    link(V.tensor_tensor(R[:, pick, :, :], R[:, pick, :, :], order16, ALU.mult))
                    link(V.tensor_reduce(mx, R[:, pick, :, :], AX.X, ALU.max))
                    link(V.tensor_tensor(R[:, pick, :, :], R[:, pick, :, :], wide(mx), ALU.is_equal))
                    if pick == 2:
                        link(V.scalar_tensor_tensor(out=R[:, 1, :, :], in0=R[:, pick, :, :], scalar=-2e30,
                                                    in1=R[:, 1, :, :], op0=ALU.mult, op1=ALU.add))
                V.tensor_tensor(R[:, 2, :, :], R[:, 2, :, :], R[:, 3, :, :], ALU.add).then_inc(rank_in, 1)
                dve.wait_ge(rank_in, layer + 1)
                link(V.tensor_tensor(R[:, 3, :, :], R[:, 2, :, :], R[:, 0, :, :], ALU.mult))
                link(V.tensor_reduce(sm, R[:, 3, :, :], AX.X, ALU.add))
                link(V.reciprocal(sm, sm))
                link(V.tensor_tensor(R[:, 4, :, :], R[:, 3, :, :], wide(sm), ALU.mult))

            def moe(layer):
                turn_h(f"mix_turn{layer}_")
                routing(layer)
                first, more = passes[layer]
                wait_ready(dve, f"rank{layer}", 4)
                counts = bank[4][:, 0:3 * EXPERTS].rearrange("p (t e) -> p t e", e=EXPERTS)
                step(V.tensor_tensor(rank[:, :, :], counts[:, 0:TB, :], route[:, 2, :, :], ALU.mult))
                V.tensor_reduce(load_f[:, :], counts[:, TB, :], AX.X, ALU.max).then_inc(stored[4], 1)
                wait_stored(dve, f"rank{layer}", 4)
                V.tensor_copy(load_i[:, :], load_f[:, :]).then_inc(load_ready, 1)
                n_lists = TB * EXPERTS
                places = consts[:, C_IOTA:C_IOTA + BLOCK]

                def pick(w):
                    V.tensor_tensor(sel.rearrange("p t e n -> p (t e) n"),
                                    places.rearrange("p (o n) -> p o n", o=1).to_broadcast([P, n_lists, BLOCK]),
                                    rank.rearrange("p t e -> p (t e)").rearrange("p (l o) -> p l o", o=1)
                                    .to_broadcast([P, n_lists, BLOCK]), ALU.is_equal).then_inc(w.sel, 1)

                pick(first)
                dve.wait_ge(load_ready, layer + 1)
                load = dve.value_load(load_i[0:1, 0:1], min_val=0, max_val=SEQ)

                def experts(w, i, e0):
                    def weigh(pair):
                        for t in range(TB):
                            for e in range(2):
                                at = bass.ds(e0 * 4 + (2 * pair + e), 1)
                                ins = V.tensor_scalar(selw[:, t, e * BLOCK:(e + 1) * BLOCK], places, rank[:, t, at],
                                                      route[:, 4, t, at], ALU.is_equal, ALU.mult)
                        ins.then_inc(w.selw, 1)

                    weigh(0)
                    for b in (1, 3):
                        w.filled(dve, i, b, 0)
                        V.tensor_copy(flat(xg[:, 2 * b:2 * b + 2, :]), bank[b][:, :]).then_inc(w.stored[b], 1)
                    for pair in range(2):
                        w.read(dve, i, 2, 1 + 2 * pair)
                        w.filled(dve, i, 3, 1 + 2 * pair)
                        V.tensor_tensor(hid, sil, bank[3][:, :], ALU.mult).then_inc(w.stored[3], 1)
                        w.filled(dve, i, 1, 1 + pair)
                        V.tensor_copy(selw_t[:, pair, :], bank[1][:, 0:SEQ]).then_inc(w.stored[1], 1)
                        if pair == 0:
                            weigh(1)
                        w.filled(dve, i, 3, 2 + 2 * pair)
                        V.tensor_copy(ye[:, 512:1024], bank[3][:, :]).then_inc(w.stored[3], 1)

                with dve.Fori(0, QUADS) as i:
                    experts(first, i, i)
                with dve.If(load > BLOCK):
                    with dve.Fori(0, PASSES - 1) as p:
                        V.tensor_scalar(rank[:, :, :], rank[:, :, :], float(BLOCK), None, ALU.subtract) \
                            .then_inc(more.next, 1)
                        dve.wait_ge(more.next, p + 1)
                        pick(more)
                        with dve.Fori(0, QUADS) as i:
                            experts(more, p * QUADS + i, i)

                def add(t, half):
                    b = 4 + 2 * t + half
                    wait_ready(dve, f"ffn{layer}", b)
                    V.scalar_tensor_tensor(out=h[:, t, half * 512:(half + 1) * 512],
                                           in0=h[:, t, half * 512:(half + 1) * 512], scalar=ALPHA,
                                           in1=bank[b][:, :], op0=ALU.mult, op1=ALU.add).then_inc(stored[b], 1)
                    wait_stored(dve, f"ffn{layer}", b)
                layernorm(add, 2 * TB * layer + TB)

            moe(0)
            turn_h("ffn_turn0_")

            for u, first in ((0, 0), (1, 4)):
                for q, b in enumerate(plan[f"cd{u}"]):
                    wait_ready(dve, f"cd{u}", b)
                    V.tensor_copy(feat[:, first + 2 * q:first + 2 * q + 2, :].rearrange("p k t -> p (k t)"),
                                  bank[b][:, :]).then_inc(stored[b], 1)
            b0, b1 = plan["alpha_in"]
            G = gate_row[0:16, :, :]
            wait_ready(dve, "alpha_in", b0)
            V.tensor_copy(G[:, 0, :], bank[b0][0:16, 0:SEQ]).then_inc(stored[b0], 1)
            wait_ready(dve, "alpha_in", b1)
            V.tensor_scalar(G[:, 4, :], bank[b1][0:16, 0:SEQ], ssd_par[:, 0:1], None, ALU.add) \
                .then_inc(stored[b1], 1)
            wait_stored(dve, "alpha_in", b1)
            V.scalar_tensor_tensor(out=G[:, 1, :], in0=G[:, 4, :], scalar=-1.0, in1=G[:, 4, :], op0=ALU.mult,
                                   op1=ALU.max).then_inc(gate_a, 1)
            dve.wait_ge(gate_b, 2)
            link(V.scalar_tensor_tensor(out=G[:, 2, :], in0=G[:, 4, :], scalar=0.0, in1=G[:, 2, :],
                                        op0=ALU.max, op1=ALU.add))
            link(V.tensor_scalar(G[:, 1, :], G[:, 2, :], ssd_par[:, 1:2], -1.0, ALU.mult, ALU.mult))
            V.tensor_tensor_scan(G[:, 3, :], ones_row[0:16, :], G[:, 1, :], 0.0, ALU.mult, ALU.add) \
                .then_inc(gate_ok, 1)
            for q, b in enumerate(plan["alpha"]):
                wait_ready(dve, "alpha", b)
                for hd in (2 * q, 2 * q + 1):
                    ins = V.tensor_scalar(bcum[:, hd, :], bank[b][:, (hd % 2) * SEQ:(hd % 2 + 1) * SEQ],
                                          cols_cd[:, ROWS_CD["b_alpha"] + hd:ROWS_CD["b_alpha"] + hd + 1], None,
                                          ALU.add)
                    ins.then_inc(stored[b], 1) if hd % 2 else step(ins)
                wait_stored(dve, "alpha", b)
            V.scalar_tensor_tensor(out=gtmp, in0=bcum, scalar=-1.0, in1=bcum, op0=ALU.mult,
                                   op1=ALU.max).then_inc(gate_a, 1)
            dve.wait_ge(gate_b, 3)
            link(V.scalar_tensor_tensor(out=gtmp, in0=bcum, scalar=0.0, in1=gtmp, op0=ALU.min, op1=ALU.subtract))
            link(V.memset(dec[:, 0, 0:SEQ], 1.0))
            for hd in range(HEADS):
                link(V.tensor_tensor_scan(bcum[:, hd, :], dec[:, 0, 0:SEQ], gtmp[:, hd, :], 0.0, ALU.mult, ALU.add))
            b0 = first_of("dt_cols")
            wait_ready(dve, "dt_cols", b0)
            link(V.tensor_copy(gate_col[:, 1, :, :], bank[b0][:, 0:32].rearrange("p (t n) -> p t n", t=TB)))
            V.tensor_scalar(route[:, 5, :, :], bank[b0][:, 32:64].rearrange("p (t n) -> p t n", t=TB), -1.0,
                            None, ALU.mult).then_inc(stored[b0], 1)
            refs = gate_col[:, 0, :, :].rearrange("p a b -> p (a b)").rearrange("p (h i) -> p h i", h=HEADS)
            V.tensor_scalar(refs, bcum[:, :, GLA_MID::GLA_BLOCK], 1.0 / GLA_TAU, None, ALU.mult) \
                .then_inc(gate_a, 1)
            dve.wait_ge(gate_a, 5)

            def gla_head(hd):
                blocks = lambda x: x.rearrange("p (i c) -> p i c", c=GLA_BLOCK)
                V.tensor_tensor(blocks(dec[:, hd, 0:SEQ]), blocks(bcum[:, hd, :]),
                                bcum[:, hd, GLA_MID::GLA_BLOCK].rearrange("p (i o) -> p i o", o=1)
                                .to_broadcast([P, SEQ // GLA_BLOCK, GLA_BLOCK]), ALU.subtract).then_inc(dec_arg, 1)
                dve.wait_ge(dec_done, 8 + hd + 1)
                link(V.scalar_tensor_tensor(out=feat[:, hd, :], in0=dec[:, hd, 0:SEQ], scalar=GLA_CAP,
                                            in1=feat[:, hd, :], op0=ALU.min, op1=ALU.mult))
                for i in range(SEQ // GLA_BLOCK):
                    n = P if i < 4 else SEQ
                    k = 8 * hd + i
                    dve.wait_ge(kexp, k + 1)
                    if i >= 2:
                        dve.wait_ge(kused, 7 * hd + i - 1)
                    elif hd:
                        dve.wait_ge(kused, 7 * hd)
                        wait_ready(dve, f"s_gla{hd - 1}", first_of(f"s_gla{hd - 1}"))
                    V.scalar_tensor_tensor(out=gtmp[:, i % 2, 0:n], in0=gtmp[:, 2 + i % 2, 0:n], scalar=GLA_CAP,
                                           in1=feat[:, 4 + hd, 0:n], op0=ALU.min, op1=ALU.mult) \
                        .then_inc(kscale, 1)

            def p_gla(hd):
                b = first_of(f"s_gla{hd}")
                decayed(f"s_gla{hd}", b, hd, QK_SCALE, cmask, 0).then_inc(stored[b], 1)

            def square_mean(src):
                for t in range(TB):
                    link(V.bn_stats(stat[:, t, :], src(t)))
                    link(V.bn_aggr(mv[:, t, :], stat[:, t, :]))
                link(V.tensor_tensor(mv[:, :, 0], mv[:, :, 0], mv[:, :, 0], ALU.mult))
                V.tensor_tensor(mv[:, :, 1], mv[:, :, 1], mv[:, :, 0], ALU.add).then_inc(var_ready, 1)

            def y_gla(hd):
                b = first_of(f"y_gla{hd}")
                wait_ready(dve, f"y_gla{hd}", b)
                square_mean(lambda t: bank[b][:, t * DV:(t + 1) * DV])
                wait_root()
                cols = slice(hd * DV, (hd + 1) * DV)
                for bb in plan["cd4" if hd < 2 else "cd5"]:
                    wait_stored(dve, "cd4" if hd < 2 else "cd5", bb)
                for t in range(TB):
                    ins = V.scalar_tensor_tensor(out=tok[:, 1, t, cols], in0=bank[b][:, t * DV:(t + 1) * DV],
                                                 scalar=rstd[:, t:t + 1], in1=tok[:, 1, t, cols],
                                                 op0=ALU.mult, op1=ALU.mult)
                    ins.then_inc(stored[b], 1) if t else step(ins)

            gla_head(0)
            p_gla(0)
            gla_head(1)
            p_gla(1)
            cw = ROWS_CD["conv_w"]
            y_gla(0)
            y_gla(1)
            taps("cd6", 8, cols_cd, cw, 16, 0, 8)
            gla_head(2)
            p_gla(2)
            gla_head(3)
            p_gla(3)
            taps("cd7", 12, cols_cd, cw, 16, 4, 12)
            y_gla(2)
            y_gla(3)
            taps("cd8", 16, cols_cd, cw, 16, 8, 16)
            taps("cd9", 20, cols_cd, cw, 16, 12, 20)
            y_turns(1, cols_cd, (0, 1))
            for n in range(4):
                for q, b in enumerate(plan[f"xs_turn{n}"]):
                    wait_ready(dve, f"xs_turn{n}", b)
                    t, c0 = n // 2, 4 * (n % 2) + 2 * q
                    heads = lambda x: x.rearrange("p (n d) -> p n d", d=SSD_HD)
                    nh = 2 * P // SSD_HD
                    h0 = c0 * P // SSD_HD
                    wide = lambda x: x.rearrange("p (n o) -> p n o", o=1).to_broadcast([P, nh, SSD_HD])
                    link(V.tensor_tensor(heads(tok[:, 2, t, c0 * P:(c0 + 2) * P]), heads(bank[b][:, 0:2 * P]),
                                         wide(ssd_d[:, h0:h0 + nh]), ALU.mult))
                    V.tensor_tensor(heads(xdt[:, t, c0 * P:(c0 + 2) * P]), heads(bank[b][:, 0:2 * P]),
                                    wide(gate_col[:, 1, t, h0:h0 + nh]), ALU.mult).then_inc(stored[b], 1)
            for g in range(GROUPS):
                decay_args(f"cum{g}", lambda r, j: route[:, 5, j, 4 * g + r:4 * g + r + 1],
                           lambda r: ssd_dec[:, r, :], 0)
                sbk, yb = first_of(f"s_ssd{g}"), first_of(f"y_ssd{g}")
                for r in range(4):
                    hd = 4 * g + r
                    if r >= 2:
                        dve.wait_ge(kused, 28 + 3 * g + r - 1)
                    elif g:
                        dve.wait_ge(kused, 28 + 3 * g)
                        wait_ready(dve, f"y_ssd{g - 1}", first_of(f"y_ssd{g - 1}"))
                    ins = decayed(f"s_ssd{g}", sbk, hd, 1.0, ssd_dec[:, r, :], 12 + hd + 1)
                    ins.then_inc(prob_ready if r < 3 else stored[sbk], 1)
                wait_ready(dve, f"y_ssd{g}", yb)
                cols = slice(g * DV, (g + 1) * DV)
                if g == 0:
                    for u in (10, 11):
                        for bb in plan[f"cd{u}"]:
                            wait_stored(dve, f"cd{u}", bb)
                for t in range(TB):
                    ins = V.tensor_tensor(tok[:, 2, t, cols], bank[yb][:, t * DV:(t + 1) * DV],
                                          tok[:, 2, t, cols], ALU.add)
                    ins.then_inc(stored[yb], 1) if t else step(ins)
                wait_stored(dve, f"y_ssd{g}", yb)
                for t in range(TB):
                    link(V.tensor_tensor(tok[:, 3, t, cols], tok[:, 3, t, cols], tok[:, 2, t, cols], ALU.mult))
                square_mean(lambda t: tok[:, 3, t, cols])
                wait_root()
                for t in range(TB):
                    ins = V.tensor_scalar(tok[:, 3, t, cols], tok[:, 3, t, cols], rstd[:, t:t + 1], None, ALU.mult)
                    link(ins) if t == 0 else ins.then_inc(y_done, 1)
                dve.wait_ge(y_done, 8 + g + 1)
            y_turns(1, cols_cd, (2, 3))
            layernorm(add_mix(1), 2 * TB)
            moe(1)


_INS = ["x", "positions", "w_in_ab", "ret_norm_g", "ml_conv_w", "ml_conv_b", "ml_b_i", "ml_b_f", "ml_norm_g",
        "w_out_ab", "w_in_cd", "gla_w_alpha", "gla_b_alpha", "gla_norm_g", "ssd_conv_w", "ssd_conv_b",
        "ssd_dt_bias", "ssd_a_log", "ssd_d", "ssd_norm_g", "w_out_cd", "w_router", "b_router", "moe_w_gate",
        "moe_w_up", "moe_w_down", "ln_mix_g", "ln_mix_b", "ln_ffn_g", "ln_ffn_b"]


def kernel(**inputs):
    import concourse.bacc as _bacc
    from concourse.bass_utils import run_bass_kernel_spmd as _run

    nc = _bacc.Bacc("TRN2", target_bir_lowering=False, num_devices=1)
    arrays, aps = {}, {}
    for name in _INS + ["consts"]:
        v = np.ascontiguousarray(shape_constants() if name == "consts" else inputs[name])
        arrays[f"in_{name}"] = v
        aps[name] = nc.dram_tensor(f"in_{name}", v.shape, mybir.dt.from_np(v.dtype), kind="ExternalInput").ap()
    out = nc.dram_tensor("out_0", (1, SEQ, D), F32, kind="ExternalOutput").ap()
    build(nc, aps, out)
    r = _run(nc, [arrays], core_ids=[0])
    return r.results[0]["out_0"]
```
